# Optimizing a Trainium2 kernel written in Bass

```python
import math
import jax, jax.numpy as jnp
from jax import lax
import numpy as np

D_MODEL = 1024
BATCH = 1
SEQ = 512
DEPTH = 2
DEC_BATCH = 8
DEC_SEQ = 4
PAST_LEN = 512
PAGE_SIZE = 128

SSM_EXPAND = 2
D_INNER = SSM_EXPAND * D_MODEL
SSM_HEAD_DIM = 64
SSM_HEADS = D_INNER // SSM_HEAD_DIM
SSM_GROUPS = 8
SSM_STATE = 128
CONV_WIDTH = 4
CONV_DIM = D_INNER + 2 * SSM_GROUPS * SSM_STATE
SSD_CHUNK = 128
ATTN_HEAD_DIM = 64
DIL_PATTERNS = ((128, 1), (512, 4), (2048, 16))
HEADS_PER_GROUP = 4
ATTN_HEADS = HEADS_PER_GROUP * len(DIL_PATTERNS)
ATTN_WIDTH = ATTN_HEADS * ATTN_HEAD_DIM
ATTN_OUT_WIDTH = HEADS_PER_GROUP * ATTN_HEAD_DIM
ROPE_DIM = ATTN_HEAD_DIM // 4
ROPE_THETA = 500000.0
Q_BLOCK = 128
D_FF = 4 * D_MODEL
DEEPNORM_ALPHA = (2 * DEPTH) ** 0.25
DEEPNORM_BETA = (8 * DEPTH) ** -0.25
LN_EPS = 1e-5
RMS_EPS = 1e-5
OFF_XBC = D_INNER
OFF_DT = OFF_XBC + CONV_DIM
OFF_Q = OFF_DT + SSM_HEADS
OFF_K = OFF_Q + ATTN_WIDTH
OFF_V = OFF_K + ATTN_WIDTH
OFF_G = OFF_V + ATTN_WIDTH
D_IN_PROJ = OFF_G + 2 * D_MODEL

kernel_name = 'hybrid_ssd_dilated_attn_deepnorm_step'

def layer_norm(x, g, b):
    xf = x.astype(jnp.float32)
    mu = jnp.mean(xf, -1, keepdims=True)
    var = jnp.mean(jnp.square(xf - mu), -1, keepdims=True)
    return ((xf - mu) * lax.rsqrt(var + LN_EPS) * g.astype(jnp.float32) + b.astype(jnp.float32)).astype(x.dtype)

def apply_partial_rotary(x, pos):
    half = ROPE_DIM // 2
    inv_freq = jnp.power(ROPE_THETA, -jnp.arange(half, dtype=jnp.float32) / half)
    ang = pos.astype(jnp.float32)[:, None] * inv_freq[None, :]
    cos = jnp.cos(ang)[None, :, None, :]
    sin = jnp.sin(ang)[None, :, None, :]
    xr = x[..., :ROPE_DIM].astype(jnp.float32)
    x1, x2 = xr[..., :half], xr[..., half:]
    rot = jnp.concatenate([x1 * cos - x2 * sin, x2 * cos + x1 * sin], -1).astype(x.dtype)
    return jnp.concatenate([rot, x[..., ROPE_DIM:]], -1)

def dilated_group_attention(q, kv, q_offset, dilation, n_keys):
    bsz, lq, nh, hd = q.shape
    qb = min(Q_BLOCK, lq)
    nb = lq // qb
    scale = 1.0 / math.sqrt(hd)
    q_blocks = q.reshape(bsz, nb, qb, nh, hd).swapaxes(0, 1)
    steps = dilation * jnp.arange(n_keys)

    def one_block(args):
        qblk, blk = args
        qi = q_offset + blk * qb + jnp.arange(qb)
        idx = qi[:, None] - steps[None, :]
        valid = idx >= 0
        kvg = jnp.take(kv, jnp.maximum(idx, 0), axis=1).astype(jnp.float32)
        s = jnp.einsum('bqhd,bqkhd->bqhk', qblk.astype(jnp.float32), kvg[:, :, :, 0]) * scale
        s = jnp.where(valid[None, :, None, :], s, -jnp.inf)
        lse = jax.nn.logsumexp(s, axis=-1)
        p = jnp.exp(s - lse[..., None])
        o = jnp.einsum('bqhk,bqkhd->bqhd', p, kvg[:, :, :, 1])
        return o, lse

    o, lse = lax.map(one_block, (q_blocks, jnp.arange(nb)))
    o = o.swapaxes(0, 1).reshape(bsz, lq, nh, hd)
    lse = lse.swapaxes(0, 1).reshape(bsz, lq, nh)
    return o, lse

def dilated_mixture_attention(q, k, v, pos, kv_bufs):
    bsz, seqlen = q.shape[:2]
    q = apply_partial_rotary(q, pos)
    k = apply_partial_rotary(k, pos)
    outs, lses, kv_rows = [], [], []
    for j, (window, dilation) in enumerate(DIL_PATTERNS):
        hs = slice(j * HEADS_PER_GROUP, (j + 1) * HEADS_PER_GROUP)
        kv_g = jnp.stack([k[:, :, hs], v[:, :, hs]], axis=2)
        if kv_bufs is None:
            src, q_off = kv_g, 0
            kv_rows.append(kv_g[:, seqlen - min(window, seqlen):])
        else:
            buf = kv_bufs[j].astype(kv_g.dtype)
            src = jnp.concatenate([buf, kv_g], axis=1)
            q_off = buf.shape[1]
            kv_rows.append(kv_g)
        o, lse = dilated_group_attention(q[:, :, hs], src, q_off, dilation, window // dilation + 1)
        outs.append(o)
        lses.append(lse)
    wts = jax.nn.softmax(jnp.stack(lses), axis=0)
    o = jnp.einsum('gblh,gblhd->blhd', wts, jnp.stack(outs))
    return o.reshape(bsz, seqlen, ATTN_OUT_WIDTH).astype(q.dtype), kv_rows

def causal_depthwise_conv(xbc, buf, w, b):
    seqlen = xbc.shape[1]
    xp = jnp.concatenate([buf.astype(xbc.dtype), xbc], axis=1)
    out = b
    for tap in range(CONV_WIDTH):
        out = out + xp[:, tap:tap + seqlen] * w[tap]
    return jax.nn.silu(out), xp[:, seqlen:]

def ssd_chunked(x, dt, a, bm, cm, h0):
    bsz, seqlen, nh, hp = x.shape
    ng, ns = bm.shape[2], bm.shape[3]
    nr = nh // ng
    qc = min(SSD_CHUNK, seqlen)
    nc = seqlen // qc
    f32 = jnp.float32
    xc = x.reshape(bsz, nc, qc, ng, nr, hp).astype(f32)
    dtc = dt.reshape(bsz, nc, qc, ng, nr)
    bc = bm.reshape(bsz, nc, qc, ng, ns).astype(f32)
    cc = cm.reshape(bsz, nc, qc, ng, ns).astype(f32)
    acum = jnp.cumsum(dtc * a.reshape(ng, nr), axis=2)
    xdt = xc * dtc[..., None]
    causal = jnp.tril(jnp.ones((qc, qc), dtype=bool))[:, :, None, None]
    seg = acum[:, :, :, None] - acum[:, :, None, :]
    decay = jnp.exp(jnp.where(causal, seg, -jnp.inf))
    cb = jnp.einsum('bcign,bcjgn->bcijg', cc, bc)
    y_diag = jnp.einsum('bcijgr,bcjgrp->bcigrp', cb[..., None] * decay, xdt)
    decay_end = jnp.exp(acum[:, :, -1:] - acum)
    states = jnp.einsum('bcjgn,bcjgrp->bcgrpn', bc, xdt * decay_end[..., None])
    chunk_decay = jnp.exp(acum[:, :, -1])

    def step(h, inp):
        s, dec = inp
        return h * dec[..., None, None] + s, h

    h_init = h0.astype(f32).reshape(bsz, ng, nr, hp, ns)
    h_final, h_prev = lax.scan(step, h_init, (states.swapaxes(0, 1), chunk_decay.swapaxes(0, 1)))
    h_prev = h_prev.swapaxes(0, 1)
    y_off = jnp.einsum('bcign,bcgrpn->bcigrp', cc, h_prev) * jnp.exp(acum)[..., None]
    y = (y_diag + y_off).reshape(bsz, seqlen, nh, hp)
    return y, h_final.reshape(bsz, nh, hp, ns)

def ssd_mixer(z, xbc, dt_raw, conv_buf, h0, conv_w, conv_b, dt_bias, a_log, d_skip, ssm_norm_g):
    bsz, seqlen = z.shape[:2]
    xbc, conv_new = causal_depthwise_conv(xbc, conv_buf, conv_w, conv_b)
    gn = SSM_GROUPS * SSM_STATE
    xs = xbc[..., :D_INNER].reshape(bsz, seqlen, SSM_HEADS, SSM_HEAD_DIM)
    bm = xbc[..., D_INNER:D_INNER + gn].reshape(bsz, seqlen, SSM_GROUPS, SSM_STATE)
    cm = xbc[..., D_INNER + gn:].reshape(bsz, seqlen, SSM_GROUPS, SSM_STATE)
    dt = jax.nn.softplus(dt_raw.astype(jnp.float32) + dt_bias.astype(jnp.float32))
    a = -jnp.exp(a_log.astype(jnp.float32))
    y, h_new = ssd_chunked(xs, dt, a, bm, cm, h0)
    y = y + d_skip.astype(jnp.float32)[:, None] * xs.astype(jnp.float32)
    hgt = y.reshape(bsz, seqlen, D_INNER) * jax.nn.silu(z.astype(jnp.float32))
    hg = hgt.reshape(bsz, seqlen, SSM_GROUPS, D_INNER // SSM_GROUPS)
    hg = hg * lax.rsqrt(jnp.mean(hg * hg, -1, keepdims=True) + RMS_EPS)
    out = hg.reshape(bsz, seqlen, D_INNER) * ssm_norm_g.astype(jnp.float32)
    return out.astype(z.dtype), conv_new, h_new

def decoder_layer(x, pos0, kv_bufs, conv_buf, h0, w_in, conv_w, conv_b, dt_bias, a_log, d_skip,
                  ssm_norm_g, w_ssm_br, w_attn_br, w_o, ln1_g, ln1_b, w_up, w_down, ln2_g, ln2_b):
    bsz, seqlen, _ = x.shape
    proj = jnp.einsum('bld,de->ble', x, w_in)
    z = proj[..., :OFF_XBC]
    xbc = proj[..., OFF_XBC:OFF_DT]
    dt_raw = proj[..., OFF_DT:OFF_Q]
    q = proj[..., OFF_Q:OFF_K].reshape(bsz, seqlen, ATTN_HEADS, ATTN_HEAD_DIM)
    k = proj[..., OFF_K:OFF_V].reshape(bsz, seqlen, ATTN_HEADS, ATTN_HEAD_DIM)
    v = proj[..., OFF_V:OFF_G].reshape(bsz, seqlen, ATTN_HEADS, ATTN_HEAD_DIM)
    gate_ssm = jax.nn.sigmoid(proj[..., OFF_G:OFF_G + D_MODEL])
    gate_attn = jax.nn.sigmoid(proj[..., OFF_G + D_MODEL:])
    if conv_buf is None:
        conv_buf = jnp.zeros((bsz, CONV_WIDTH - 1, CONV_DIM), x.dtype)
        h0 = jnp.zeros((bsz, SSM_HEADS, SSM_HEAD_DIM, SSM_STATE), jnp.float32)
    y_ssm, conv_new, h_new = ssd_mixer(z, xbc, dt_raw, conv_buf, h0, conv_w, conv_b, dt_bias,
                                       a_log, d_skip, ssm_norm_g)
    pos = pos0 + jnp.arange(seqlen)
    o_attn, kv_rows = dilated_mixture_attention(q, k, v, pos, kv_bufs)
    merged = gate_ssm * jnp.einsum('ble,ed->bld', y_ssm, w_ssm_br) \
        + gate_attn * jnp.einsum('ble,ed->bld', o_attn, w_attn_br)
    mix = jnp.einsum('bld,de->ble', merged, w_o)
    x = layer_norm(DEEPNORM_ALPHA * x + mix, ln1_g, ln1_b)
    hid = jnp.square(jax.nn.relu(jnp.einsum('bld,df->blf', x, w_up)))
    x = layer_norm(DEEPNORM_ALPHA * x + jnp.einsum('blf,fd->bld', hid, w_down), ln2_g, ln2_b)
    return x, kv_rows, conv_new, h_new

def setup_inputs(seed: int = 0) -> dict:
    key = jax.random.key(seed)
    ks = jax.random.split(key, 24)
    f32 = jnp.float32
    nrm = lambda k, shape, s: jax.random.normal(k, shape, f32) * s
    win_lens = [min(w, PAST_LEN) for (w, _) in DIL_PATTERNS]
    col_scale = jnp.concatenate([jnp.ones((OFF_V,), f32),
                                 jnp.full((ATTN_WIDTH,), DEEPNORM_BETA, f32),
                                 jnp.ones((D_IN_PROJ - OFF_G,), f32)])
    w_in = nrm(ks[0], (DEPTH, D_MODEL, D_IN_PROJ), D_MODEL ** -0.5) * col_scale
    u = jax.random.uniform(ks[1], (DEPTH, SSM_HEADS), f32)
    dt0 = jnp.exp(u * (math.log(0.1) - math.log(0.001)) + math.log(0.001))
    dt_bias = dt0 + jnp.log(-jnp.expm1(-dt0))
    a_log = jnp.log(jax.random.uniform(ks[2], (DEPTH, SSM_HEADS), f32, 1.0, 16.0))
    return {
        'x_prompt': nrm(ks[3], (BATCH, SEQ, D_MODEL), 1.0),
        'x_sample': nrm(ks[4], (DEC_BATCH, DEC_SEQ, D_MODEL), 1.0),
        'cache_kv_w128': nrm(ks[5], (DEPTH, DEC_BATCH, win_lens[0], 2, HEADS_PER_GROUP, ATTN_HEAD_DIM), 1.0),
        'cache_kv_w512': nrm(ks[6], (DEPTH, DEC_BATCH, win_lens[1], 2, HEADS_PER_GROUP, ATTN_HEAD_DIM), 1.0),
        'cache_kv_w2048': nrm(ks[7], (DEPTH, DEC_BATCH, win_lens[2], 2, HEADS_PER_GROUP, ATTN_HEAD_DIM), 1.0),
        'state_conv': nrm(ks[8], (DEPTH, DEC_BATCH, CONV_WIDTH - 1, CONV_DIM), 1.0),
        'state_ssm': nrm(ks[9], (DEPTH, DEC_BATCH, SSM_HEADS, SSM_HEAD_DIM, SSM_STATE), 0.1),
        'w_in': w_in,
        'conv_w': nrm(ks[10], (DEPTH, CONV_WIDTH, CONV_DIM), CONV_WIDTH ** -0.5),
        'conv_b': nrm(ks[11], (DEPTH, CONV_DIM), 0.01),
        'dt_bias': dt_bias,
        'a_log': a_log,
        'd_skip': 1.0 + nrm(ks[12], (DEPTH, SSM_HEADS), 0.01),
        'ssm_norm_g': 1.0 + nrm(ks[13], (DEPTH, D_INNER), 0.01),
        'w_ssm_br': nrm(ks[14], (DEPTH, D_INNER, D_MODEL), D_INNER ** -0.5),
        'w_attn_br': nrm(ks[15], (DEPTH, ATTN_OUT_WIDTH, D_MODEL), ATTN_OUT_WIDTH ** -0.5),
        'w_o': nrm(ks[16], (DEPTH, D_MODEL, D_MODEL), D_MODEL ** -0.5 * DEEPNORM_BETA),
        'ln1_g': 1.0 + nrm(ks[17], (DEPTH, D_MODEL), 0.01),
        'ln1_b': nrm(ks[18], (DEPTH, D_MODEL), 0.01),
        'w_up': nrm(ks[19], (DEPTH, D_MODEL, D_FF), D_MODEL ** -0.5),
        'w_down': nrm(ks[20], (DEPTH, D_FF, D_MODEL), D_FF ** -0.5 * DEEPNORM_BETA),
        'ln2_g': 1.0 + nrm(ks[21], (DEPTH, D_MODEL), 0.01),
        'ln2_b': nrm(ks[22], (DEPTH, D_MODEL), 0.01),
    }

def reference(x_prompt, x_sample, cache_kv_w128, cache_kv_w512, cache_kv_w2048, state_conv, state_ssm,
              w_in, conv_w, conv_b, dt_bias, a_log, d_skip, ssm_norm_g, w_ssm_br, w_attn_br, w_o,
              ln1_g, ln1_b, w_up, w_down, ln2_g, ln2_b):
    kv_caches = (cache_kv_w128, cache_kv_w512, cache_kv_w2048)
    xp, xs = x_prompt, x_sample
    p_kv = ([], [], [])
    s_kv = ([], [], [])
    p_conv, p_ssm, s_conv, s_ssm = [], [], [], []
    for l in range(DEPTH):
        params = (w_in[l], conv_w[l], conv_b[l], dt_bias[l], a_log[l], d_skip[l], ssm_norm_g[l],
                  w_ssm_br[l], w_attn_br[l], w_o[l], ln1_g[l], ln1_b[l], w_up[l], w_down[l],
                  ln2_g[l], ln2_b[l])
        xp, kv_rows, conv_new, h_new = decoder_layer(xp, 0, None, None, None, *params)
        for j in range(len(DIL_PATTERNS)):
            p_kv[j].append(kv_rows[j])
        p_conv.append(conv_new)
        p_ssm.append(h_new.astype(xp.dtype))
        bufs = (kv_caches[0][l], kv_caches[1][l], kv_caches[2][l])
        xs, kv_rows, conv_new, h_new = decoder_layer(xs, PAST_LEN, bufs, state_conv[l], state_ssm[l], *params)
        for j in range(len(DIL_PATTERNS)):
            s_kv[j].append(kv_rows[j])
        s_conv.append(conv_new)
        s_ssm.append(h_new.astype(state_ssm.dtype))
    return (xp, xs,
            jnp.stack(p_kv[0]), jnp.stack(p_kv[1]), jnp.stack(p_kv[2]), jnp.stack(p_conv), jnp.stack(p_ssm),
            jnp.stack(s_kv[0]), jnp.stack(s_kv[1]), jnp.stack(s_kv[2]), jnp.stack(s_conv), jnp.stack(s_ssm))


_drawn_inputs = setup_inputs


def setup_inputs(seed=0):
    import zlib

    import numpy as np

    out = dict(_drawn_inputs(seed))
    spreads = {}
    factors = {'cache_kv_w128': 3.126,
     'cache_kv_w512': 3.177,
     'cache_kv_w2048': 6.239,
     'conv_b': 3.658,
     'd_skip': 34.67,
     'ssm_norm_g': 25.651,
     'ln1_g': 3.752,
     'ln1_b': 3.868,
     'ln2_g': 3.77,
     'ln2_b': 3.808}
    for name, (base, spread) in spreads.items():
        noise = np.random.default_rng([zlib.crc32(name.encode()), seed]).standard_normal(out[name].shape)
        drawn = base * np.exp(spread * noise) if base else spread * noise
        out[name] = __import__('jax').numpy.asarray(drawn.astype(out[name].dtype))
    for name, factor in factors.items():
        out[name] = (out[name] * factor).astype(out[name].dtype)
    return out
```

```python
from contextlib import ExitStack

import numpy as np

import concourse.bass as bass
from concourse import mybir

F32 = mybir.dt.float32
BF16 = mybir.dt.bfloat16
U16 = mybir.dt.uint16
ALU = mybir.AluOpType
ACT = mybir.ActivationFunctionType
AX_X = mybir.AxisListType.X

P = 128
DEPTH, D = 2, 1024
SEQ, NB, NS = 512, 8, 4
TS = NB * NS
T = SEQ + TS
HT = T // 2
KT = D // P
HEADS, GROUPS, HD, NST = 32, 8, 64, 128
HG = HEADS // GROUPS
CHUNK = 128
NC = SEQ // CHUNK
CW = 4
D_IN = HEADS * HD
CONV = D_IN + 2 * GROUPS * NST
AW = 768
OFF_XBC, OFF_DT = D_IN, D_IN + CONV
OFF_Q = OFF_DT + HEADS
OFF_K, OFF_V, OFF_G = OFF_Q + AW, OFF_Q + 2 * AW, OFF_Q + 3 * AW
DFF = 4 * D
FT = DFF // P // 2
ALPHA = (2 * DEPTH) ** 0.25
EPS = 1e-5
PAST = 512
WINDOWS = ((128, 1), (512, 4), (2048, 16))
ROPE, THETA = 16, 500000.0
RES = 4
NEG = -1e30
KEYS = SEQ + 2 * P
SKEYS = KEYS + 3 * TS

SLOTS = 4
SIX = (0, 1, 2, 3, 0, 1)
U_QKV, U_GRP, U_MRG, U_WO, U_FFN, UNITS = 0, 18, 66, 98, 106, 170
B_QKV = (0, 0, 0, 0)
B_GRP = (6, 6, 3, 3)
B_MRG = (22, 22, 11, 11)
B_WO = (30, 30, 19, 19)
B_FFN = (32, 32, 21, 21)
B_ALL = (48, 48, 37, 37)

T_DT, T_QKV, T_ATT, T_SMP, T_GRP, T_MRG, T_WO, T_FFN, TILES = 0, 1, 19, 35, 36, 84, 116, 124, 172
N_DT, N_ATT, N_SMP, N_MRG, COUNTED = 0, 1, 17, 18, 26

NGP = 4 * CW + 4 + 2 + 2
HP_N = 32


def six(L, base, i, k):
    s = SIX[k]
    return s, L * B_ALL[s] + base[s] + i * (2 if s < 2 else 1) + k // SLOTS


def four(L, base, i, k):
    return k, L * B_ALL[k] + base[k] + i


def build(nc, A):
    with ExitStack() as ctx:
        def sb(name, shape, dt=F32):
            return ctx.enter_context(nc.sbuf_tensor(name, shape, dt))

        def sem(name):
            return ctx.enter_context(nc.semaphore(name))

        class Region:

            def __init__(self, name, words):
                self.t, self.words, self.at, self.high = sb(name, [P, words]), words, 0, 0

            def take(self, *dims, parts=P):
                n = int(np.prod(dims))
                v = self.t[0:parts, self.at:self.at + n]
                self.at += n
                assert self.at <= self.words, (self.at, self.words)
                self.high = max(self.high, self.at)
                if len(dims) == 2:
                    v = v.rearrange("p (a b) -> p a b", a=dims[0])
                if len(dims) == 3:
                    v = v.rearrange("p (a b c) -> p a b c", a=dims[0], b=dims[1])
                if len(dims) == 4:
                    v = v.rearrange("p (a b c d) -> p a b c d", a=dims[0], b=dims[1], c=dims[2])
                return v

            def restart(self, at=0):
                self.at = at

        xT = sb("xT", [P, KT, T])
        wring = sb("wring", [P, SLOTS, KT * P])
        oT = sb("oT", [P, 2, T])
        ident = sb("ident", [P, P])
        ones = sb("ones", [P, P])
        swap = sb("swap", [P, P])
        cosT = sb("cosT", [P, T])
        sinT = sb("sinT", [P, T])
        tri = sb("tri", [P, P])
        tri_s = sb("tri_s", [TS, TS])
        bmask = sb("bmask", [TS, NB])
        restart = sb("restart", [HEADS, T])
        wdt = sb("wdt", [P, KT, HEADS])
        par = sb("par", [P, GROUPS, NGP])
        lnp = sb("lnp", [P, HP_N])
        hpar = sb("hpar", [HEADS, 2])
        cst = sb("cst", [P, 4 * GROUPS, NB * (CW - 1)])
        tokm = sb("tokm", [P, NC + 1, 3, HEADS])
        gp = sb("gp", [P, NGP - 20])
        gconv = sb("gconv", [P, 20])
        gt = sb("gt", [P, NC + 1, 3, HG])
        eps = sb("eps", [P, 1])
        dtv = [sb(f"dtv{i}", [HEADS, T]) for i in range(3)]
        dt_t, ac_t, de_t = dtv
        a_col = sb("a_col", [HEADS, 1])

        big = Region("big", D_IN // P * T)
        yssm = big.take(D_IN // P, T)
        hid = yssm
        big.restart()
        d_e, d_r, d_z, d_z2 = (big.take(T, parts=HEADS) for _ in range(4))
        cring = big.take(4, 12 * P)
        big.restart()

        reg = Region("region", 25600)
        qkvT = reg.take(18, T)
        rraw = reg.take(2, T)
        rtmp = reg.take(T)
        vtok = reg.take(NC, 256)
        vtok_s = reg.take(AW, parts=TS)
        mask = reg.take(RES, KEYS // 2).bitcast(BF16)
        mask_s = reg.take(SKEYS // 2).bitcast(BF16)
        qz = reg.take(3, HG, P)
        kr = reg.take(4, P)
        vr = reg.take(4, P)
        v_res = reg.take(4, P)
        sc = reg.take(2, KEYS)
        pt = reg.take(KEYS)
        rowmax = reg.take(HG)
        rowsum = reg.take(HG)
        rowinv = reg.take(HG)
        ob = reg.take(256)
        qzs = reg.take(3, 2, NB, 32)
        sc_s = reg.take(SKEYS)
        ptz = reg.take(2, 6, P)
        ptn = reg.take(3, P, parts=TS)
        reg.restart()
        st = reg.take(NB, 256)
        hst = reg.take(256)
        cout = reg.take(4, 35)
        after_stores = reg.at
        raw = reg.take(6, T)
        post = reg.take(4, T)
        th = reg.take(2, T)
        thz = reg.take(2, T)
        zs = reg.take(2, T)
        acb = reg.take(HG, T)
        ea = reg.take(HG, T)
        seg = reg.take(2, HG, P)
        mdec = reg.take(HG, P)
        cea = reg.take(HG, P)
        xdt = reg.take(256)
        xde = reg.take(256)
        btok = reg.take(P)
        cbm = reg.take(P)
        bm = reg.take(NB, P, parts=TS)
        yg = reg.take(2, T)
        sqb = reg.take(2, T)
        rsb = reg.take(T)
        spad = reg.take(4, NB * (CW - 1 + NS))
        reg.restart(after_stores)
        merged = reg.take(KT, T)
        wab = reg.take(2, P)
        gates = reg.take(2, T)
        prod = reg.take(2, T)
        part = reg.take(KT, T)
        lsq = reg.take(2, T)
        mean = reg.take(T)
        sdev = reg.take(T)
        rstd = reg.take(T)

        acc = [ctx.enter_context(nc.psum_tensor(f"acc{i}", [P, 1024], F32)) for i in range(2)]
        px = ctx.enter_context(nc.psum_tensor("px", [P, 2048], F32))
        px01, px23 = px[:, 0:1024], px[:, 1024:2048]
        X = [px[:, 512 * j:512 * (j + 1)] for j in range(4)]

        def halves(ap):
            return ap.rearrange("p (h n) -> p h n", h=2)

        def two(ps, parts=P):
            return ps[0:parts, :].rearrange("p (h n) -> p h n", h=2)[:, :, 0:HT]

        px_mid = two(px[:, 512:1536])

        def bc(ap, n):
            return ap.unsqueeze(len(ap.shape)).to_broadcast(list(ap.shape) + [n])

        const_ld = sem("const_ld")
        const_set = sem("const_set")
        w_loaded = [sem(f"w_loaded{i}") for i in range(SLOTS)]
        w_used = [sem(f"w_used{i}") for i in range(SLOTS)]
        acc_done = sem("acc_done")
        acc_free = [sem(f"acc_free{i}") for i in range(2)]
        x_ready = sem("x_ready")
        lay_ld = sem("lay_ld")
        dt_exp, dt_scan, de_ready, tok_t, tok_ready = (sem(n) for n in ("dt_exp", "dt_scan", "de_ready", "tok_t", "tok_ready"))
        ac_stored = sem("ac_stored")
        rope_raw, rope_sw, rope_px, rope_done = (sem(n) for n in ("rope_raw", "rope_sw", "rope_px", "rope_done"))
        kv_st = sem("kv_st")
        mask_ld, zeroed, qzs_ready = sem("mask_ld"), sem("zeroed"), sem("qzs_ready")
        vt_t, vt_done = sem("vt_t"), sem("vt_done")
        staged, vr_t, vr_done = sem("staged"), sem("vr_t"), sem("vr_done")
        s_max, s_exp, pt_t, pt_done, pv_done, o_norm, ot_t, ot_done = (
            sem(n) for n in ("s_max", "s_exp", "pt_t", "pt_done", "pv_done", "o_norm", "ot_t", "ot_done"))
        c_loaded = [sem(f"c_loaded{i}") for i in range(4)]
        c_used = sem("c_used")
        ss_max, ss_exp, ss_norm, spt_t, spt_done, spv_done, so_copy, so_t, att_done = (
            sem(n) for n in ("ss_max", "ss_exp", "ss_norm", "spt_t", "spt_done", "spv_done", "so_copy", "so_t", "att_done"))
        acb_ld, st_ld = sem("acb_ld"), sem("st_ld")
        gp_ready, post_init, conv_done, th_ready, post_ready, spad_ready, thz_ready, zs_done = (
            sem(n) for n in ("gp_ready", "post_init", "conv_done", "th_ready", "post_ready", "spad_ready",
                             "thz_ready", "zs_done"))
        ea_ready, seg_ready, e_ready, t_done, x0_free, m_ready, pool_step, y_done, h_ready = (
            sem(n) for n in ("ea_ready", "seg_ready", "e_ready", "t_done", "x0_free", "m_ready", "pool_step", "y_done",
                             "h_ready"))
        y_evac, gated, sq_ready, rms_sum, rs_ready, yssm_ready = (
            sem(n) for n in ("y_evac", "gated", "sq_ready", "rms_sum", "rs_ready", "yssm_ready"))
        ns_done, st_dec, ns_add, bm_ready = (sem(n) for n in ("ns_done", "st_dec", "ns_add", "bm_ready"))
        h_st, st_st, cout_st, h_free = (sem(n) for n in ("h_st", "st_st", "cout_st", "h_free"))
        wab_ld, gate_th, mrg_done = sem("wab_ld"), sem("gate_th"), sem("mrg_done")
        relu_done, hid_ready, part_done = sem("relu_done"), sem("hid_ready"), sem("part_done")
        ln_x, ln_sum, ln_mean, ln_c, ln_sq, ln_sqf, ln_sd, ln_n = (
            sem(n) for n in ("ln_x", "ln_sum", "ln_mean", "ln_c", "ln_sq", "ln_sqf", "ln_sd", "ln_n"))
        y_st = sem("y_st")
        passed = sem("passed")

        def read_of(L, base, pairs, k):
            return L * (TILES // 2) + pairs + (base + k) // 2 + 2

        def hold(eng, s, n):
            eng.wait_ge(s, n)
            eng.sem_inc(passed, 1)

        block = ctx.enter_context(nc.Block())

        @block.sync
        def _(sp):
            sp.dma_start(xT[:, :, :], A["x0"]).then_inc(x_ready, 16)
            for name, t in (("ident", ident), ("swap", swap), ("cos", cosT), ("sin", sinT), ("tri", tri),
                            ("tri_s", tri_s), ("bmask", bmask), ("restart", restart)):
                sp.dma_start(t[:, :], A[name]).then_inc(const_ld, 16)

            def load(L, unit, slot_use):
                slot, use = slot_use
                sp.wait_ge(w_used[slot], use + 1)
                sp.dma_start(wring[:, slot, :], A["wst"][bass.ds(L * UNITS + unit, 1)].rearrange("u p n -> (u p) n"))\
                  .then_inc(w_loaded[slot], 16)

            with sp.Fori(0, DEPTH) as L:
                with sp.Fori(0, 3) as i:
                    for k in range(6):
                        load(L, U_QKV + i * 6 + k, six(L, B_QKV, i, k))
                with sp.Fori(0, GROUPS) as g:
                    for k in range(6):
                        load(L, U_GRP + g * 6 + k, six(L, B_GRP, g, k))
                with sp.Fori(0, KT) as m:
                    for k in range(SLOTS):
                        load(L, U_MRG + m * 4 + k, four(L, B_MRG, m, k))
                with sp.Fori(0, 2) as i:
                    for k in range(SLOTS):
                        load(L, U_WO + i * 4 + k, four(L, B_WO, i, k))
                with sp.Fori(0, 16) as i:
                    for k in range(SLOTS):
                        load(L, U_FFN + i * 4 + k, four(L, B_FFN, i, k))
            sp.wait_ge(x_ready, 16 * (DEPTH + 1))
            sp.dma_start(A["y"], xT[:, :, :]).then_inc(y_st, 16)
            sp.wait_ge(y_st, 16)

        @block.tensor
        def _(pe):
            pe.wait_ge(const_ld, 16 * 8)
            pe.wait_ge(const_set, 3)

            def claim(L, base, pairs, k):
                pe.wait_ge(acc_free[(base + k) % 2], read_of(L, base, pairs, k) - 1)
                return (base + k) % 2

            def x_half(k, h):
                return xT[:, k, h * HT:(h + 1) * HT]

            def gemm(L, base, pairs, k, units, rhs, between=None):
                buf = claim(L, base, pairs, k)
                for j, (slot, use) in enumerate(units):
                    pe.wait_ge(w_loaded[slot], 16 * (use + 1))
                    for kk in range(KT):
                        for h in range(2):
                            mm = nc.tensor.matmul(acc[buf][:, 512 * h:512 * h + HT],
                                                  wring[:, slot, kk * P:(kk + 1) * P], rhs(8 * j + kk, h),
                                                  start=j == 0 and kk == 0,
                                                  stop=j == len(units) - 1 and kk == KT - 1)
                        if kk == KT - 1:
                            mm.then_inc(w_used[slot], 1)
                        if kk % 4 == 3 and between is not None:
                            between()

            def rope(L, idx, s):
                rho = L * 12 + idx
                pe.wait_ge(rope_raw, rho + 1)
                pe.wait_ge(rope_px, rho + 1)
                for h in range(2):
                    mm = nc.tensor.matmul(px01[:, 512 * h:512 * h + HT], swap[:, :], rraw[:, s, h * HT:(h + 1) * HT],
                                          start=True, stop=True)
                mm.then_inc(rope_sw, 1)

            def layer_norm(n):
                for k in range(KT):
                    pe.wait_ge(ln_x, 8 * n + k + 1)
                    for h in range(2):
                        mm = nc.tensor.matmul(px01[:, 512 * h:512 * h + HT], ones[:, :], x_half(k, h),
                                              start=k == 0, stop=k == KT - 1)
                mm.then_inc(ln_sum, 1)
                for k in range(KT):
                    pe.wait_ge(ln_sq, 8 * n + k + 1)
                    for h in range(2):
                        mm = nc.tensor.matmul(px23[:, 512 * h:512 * h + HT], ones[:, :],
                                              lsq[:, k % 2, h * HT:(h + 1) * HT], start=k == 0, stop=k == KT - 1)
                    mm.then_inc(ln_sqf, 1)

            with pe.Fori(0, DEPTH) as L:
                pe.wait_ge(x_ready, 16 * L + 16)
                pe.wait_ge(lay_ld, 80 * L + 80)
                buf = claim(L, T_DT, 0, 0)
                for k in range(KT):
                    for h in range(2):
                        mm = nc.tensor.matmul(acc[buf][0:HEADS, 512 * h:512 * h + HT], wdt[:, k, :], x_half(k, h),
                                              start=k == 0, stop=k == KT - 1)
                mm.then_inc(acc_done, 1)
                with pe.Fori(0, 3) as i:
                    for j in range(2):
                        for c in range(3):
                            k = 3 * j + c
                            gemm(L, T_QKV, 3 * i, k, [six(L, B_QKV, i, k)], x_half)
                            if c > 0:
                                rope(L, 4 * i + 2 * j + c - 1, c - 1)
                hold(pe, de_ready, L + 1)
                for c in range(NC + 1):
                    n = CHUNK if c < NC else TS
                    for j in range(3):
                        mm = nc.tensor.transpose(X[2][0:n, (3 * c + j) * HEADS:(3 * c + j + 1) * HEADS],
                                                 dtv[j][:, c * CHUNK:c * CHUNK + n], ident[0:HEADS, 0:HEADS])
                mm.then_inc(tok_t, 1)
                pe.wait_ge(acc_free[0], read_of(L, T_QKV, 6, 5))
                pe.wait_ge(rope_px, 12 * L + 13)
                for j in range(2):
                    for b in range(NC):
                        mm = nc.tensor.transpose(X[j][:, b * P:(b + 1) * P], qkvT[:, 12 + j, b * P:(b + 1) * P],
                                                 ident[:, :])
                    mm.then_inc(vt_t, 1)
                for j in range(4):
                    mm = nc.tensor.transpose(X[3][0:TS, j * P:(j + 1) * P], qkvT[:, 12 + j, SEQ:T], ident[:, :])
                mm.then_inc(vt_t, 1)
                pe.wait_ge(vt_done, 4 * L + 1)
                for j in range(4, 6):
                    mm = nc.tensor.transpose(X[0][0:TS, (j - 4) * P:(j - 3) * P], qkvT[:, 12 + j, SEQ:T], ident[:, :])
                mm.then_inc(vt_t, 1)
                pe.wait_ge(vt_done, 4 * L + 4)
                hold(pe, tok_ready, L + 1)
                with pe.Fori(0, RES) as r:
                    pe.wait_ge(staged, 4 * L + r + 1)
                    pe.wait_ge(ot_done, 4 * L + r + 1)
                    for j in range(4):
                        mm = nc.tensor.transpose(X[2][:, j * P:(j + 1) * P], vr[:, j, :], ident[:, :])
                    mm.then_inc(vr_t, 1)

                    def scores(h):
                        buf = claim(L, T_ATT, 2 * r, h)
                        nc.tensor.matmul(acc[buf][:, 0:SEQ], qz[:, 0, h, :], qkvT[:, 6 + h // 2, 0:SEQ],
                                         start=True, stop=True)
                        for g in (1, 2):
                            mm = nc.tensor.matmul(acc[buf][:, SEQ + (g - 1) * P:SEQ + g * P], qz[:, g, h, :],
                                                  kr[:, 2 * (g - 1) + h // 2, :], start=True, stop=True)
                        mm.then_inc(acc_done, 1)

                    def turn_probs(h):
                        pe.wait_ge(s_exp, 16 * L + 4 * r + h + 1)
                        pe.wait_ge(pt_done, 16 * L + 4 * r + h + 1)
                        for j in range(6):
                            mm = nc.tensor.transpose(px01[:, j * P:(j + 1) * P], sc[:, h % 2, j * P:(j + 1) * P],
                                                     ident[:, :])
                        mm.then_inc(pt_t, 1)

                    def values(h):
                        pe.wait_ge(pt_done, 16 * L + 4 * r + h + 2)
                        if h == 0:
                            pe.wait_ge(vr_done, 4 * L + r + 1)
                            pe.wait_ge(o_norm, 4 * L + r + 1)
                        out = X[3][:, h * HD:(h + 1) * HD]
                        for j in range(6):
                            v = (vtok[:, j, h * HD:(h + 1) * HD] if j < 4 else
                                 v_res[:, 2 * (j - 4) + h // 2, (h % 2) * HD:(h % 2 + 1) * HD])
                            mm = nc.tensor.matmul(out, pt[:, j * P:(j + 1) * P], v, start=j == 0, stop=j == 5)
                        mm.then_inc(pv_done, 1)

                    scores(0)
                    scores(1)
                    turn_probs(0)
                    scores(2)
                    values(0)
                    turn_probs(1)
                    scores(3)
                    values(1)
                    turn_probs(2)
                    values(2)
                    turn_probs(3)
                    values(3)
                    pe.wait_ge(o_norm, 4 * L + r + 2)
                    for j in range(2):
                        mm = nc.tensor.transpose(X[2][:, j * P:(j + 1) * P], ob[:, j * P:(j + 1) * P], ident[:, :])
                    mm.then_inc(ot_t, 1)
                buf = claim(L, T_SMP, 0, 0)
                pe.wait_ge(qzs_ready, L + 1)
                for bb in range(4):
                    out = acc[buf][32 * bb:32 * bb + 32, :]
                    for half in range(2):
                        b = 2 * bb + half
                        pe.wait_ge(c_loaded[b % 4], 64 * L + 16 * (b // 4) + 16)
                    terms = [(b, p) for b in (2 * bb, 2 * bb + 1) for p in range(2)]
                    for g, lo, n in ((1, 0, SEQ), (0, SEQ, P), (2, SEQ + P, P)):
                        for b, p in terms:
                            mm = nc.tensor.matmul(out[:, lo:lo + n], qzs[:, g, p, b, :],
                                                  cring[:, b % 4, p * KEYS + lo:p * KEYS + lo + n],
                                                  start=(b, p) == terms[0], stop=(b, p) == terms[-1])
                    mm.then_inc(c_used, 1)
                    for g in range(3):
                        for b, p in terms:
                            mm = nc.tensor.matmul(out[:, KEYS + g * TS:KEYS + (g + 1) * TS], qzs[:, g, p, b, :],
                                                  qkvT[:, 6 + 2 * g + p, SEQ:T],
                                                  start=(b, p) == terms[0], stop=(b, p) == terms[-1])
                mm.then_inc(acc_done, 1)
                pe.wait_ge(ss_norm, L + 1)
                pe.wait_ge(pt_done, 16 * L + 17)
                pe.wait_ge(ot_done, 4 * L + 5)
                for j in range(6):
                    nc.tensor.transpose(px01[:, j * P:(j + 1) * P], sc_s[:, j * P:(j + 1) * P], ident[:, :])
                for g in range(3):
                    mm = nc.tensor.transpose(X[2][0:TS, g * P:(g + 1) * P], sc_s[:, KEYS + g * TS:KEYS + (g + 1) * TS],
                                             ident[:, :])
                mm.then_inc(spt_t, 1)
                pe.wait_ge(spt_done, L + 1)
                hold(pe, o_norm, 4 * L + 5)
                for bb in range(4):
                    out = X[3][32 * bb:32 * bb + 32, 0:256]
                    for g in range(3):
                        nc.tensor.matmul(out, ptn[:, g, 32 * bb:32 * bb + 32], vtok_s[:, g * 256:(g + 1) * 256],
                                         start=g == 0, stop=False)
                    for half in range(2):
                        b = 2 * bb + half
                        pe.wait_ge(c_loaded[b % 4], 64 * L + 32 + 16 * (b // 4) + 16)
                        for j in range(6):
                            mm = nc.tensor.matmul(out, ptz[:, half, j, 32 * bb:32 * bb + 32],
                                                  cring[:, b % 4, j * 256:(j + 1) * 256],
                                                  start=False, stop=half == 1 and j == 5)
                    mm.then_inc(c_used, 1)
                pe.wait_ge(so_copy, L + 1)
                for j in range(2):
                    mm = nc.tensor.transpose(X[2][:, j * P:(j + 1) * P], ob[:, j * P:(j + 1) * P], ident[:, :])
                mm.then_inc(so_t, 1)

                def turn(s, c):
                    n = CHUNK if c < NC else TS
                    cols = slice(c * CHUNK, c * CHUNK + n)
                    if c == 0:
                        pe.wait_ge(post_ready, 4 * s + 4)
                    else:
                        pe.wait_ge(x0_free, 5 * s + c)
                    for j, q in enumerate((2, 3, 0)):
                        nc.tensor.transpose(X[0][0:n, j * P:(j + 1) * P], post[:, q, cols], ident[:, :])
                    nc.tensor.matmul(X[0][0:n, 384:384 + n], post[:, 0, cols], post[:, 1, cols],
                                     start=True, stop=True).then_inc(t_done, 1)

                def scan(s, c):
                    n = CHUNK if c < NC else TS
                    pe.wait_ge(m_ready, 5 * s + c + 1)
                    pe.wait_ge(pool_step, 5 * s + c + 1)
                    if 0 < c < NC:
                        pe.wait_ge(h_ready, 4 * s + c)
                    if c == NC:
                        pe.wait_ge(h_ready, 4 * s + NC)
                        pe.wait_ge(st_ld, 16 * s + 16)
                    for hh in range(HG):
                        rows = slice(HD * (hh % 2), HD * (hh % 2) + HD)
                        hcols = slice(hh * HD, (hh + 1) * HD)
                        out = (X[1 + hh // 2][rows, c * CHUNK:(c + 1) * CHUNK] if c < NC
                               else X[3][rows, 256 + TS * (hh // 2):256 + TS * (hh // 2) + TS])
                        mm = nc.tensor.matmul(out, xdt[0:n, hcols], mdec[0:n, hh, 0:n], start=True,
                                              stop=c in (0, NC))
                        if 0 < c < NC:
                            mm = nc.tensor.matmul(out, hst[:, hcols], cea[:, hh, :], start=False, stop=True)
                        if c == NC:
                            for b in range(NB):
                                mm = nc.tensor.matmul(out[:, b * NS:(b + 1) * NS], st[:, b, hcols],
                                                      cea[:, hh, b * NS:(b + 1) * NS], start=False, stop=True,
                                                      skip_group_check=True)
                    if c < NC:
                        mm = nc.tensor.matmul(X[3][:, 0:256], btok[:, :], xde[:, :], start=True, stop=True)
                    mm.then_inc(y_done, 1)

                def new_states(s, j):
                    if j == 0:
                        pe.wait_ge(x0_free, 5 * s + 5)
                        pe.wait_ge(bm_ready, s + 1)
                    if j == 1:
                        pe.wait_ge(y_evac, 2 * s + 2)
                    if j >= 2:
                        pe.wait_ge(ns_add, 4 * s + j - 1)
                    for b in (2 * j, 2 * j + 1):
                        mm = nc.tensor.matmul(X[3 * (j % 2)][:, (b % 2) * 256:(b % 2 + 1) * 256], bm[:, b, :],
                                              xde[0:TS, :], start=True, stop=True)
                    mm.then_inc(ns_done, 1)

                def rms(s):
                    pe.wait_ge(sq_ready, s + 1)
                    for j in range(2):
                        for h in range(2):
                            mm = nc.tensor.matmul(X[1 + h][:, 0:HT], ones[:, :], sqb[:, j, h * HT:(h + 1) * HT],
                                                  start=j == 0, stop=j == 1)
                    mm.then_inc(rms_sum, 1)

                def scan_steps(s, half):
                    if half < NC:
                        if half > 0:
                            scan(s, half - 1)
                        turn(s, half)
                    elif half == NC:
                        scan(s, NC - 1)
                        turn(s, NC)
                    elif half == NC + 1:
                        scan(s, NC)
                    elif half in (NC + 3, NC + 4):
                        new_states(s, 2 * (half - NC - 3))
                        new_states(s, 2 * (half - NC - 3) + 1)
                    elif half == NC + 5:
                        rms(s)

                def group(g, s):
                    done = [0]

                    def between():
                        done[0] += 1
                        if s is not None:
                            scan_steps(s, done[0])

                    if s is not None:
                        scan_steps(s, 0)
                    for k in range(6):
                        if g is not None:
                            gemm(L, T_GRP, 3 * g, k, [six(L, B_GRP, g, k)], x_half, between)
                        else:
                            between()
                            between()

                group(0, None)
                with pe.Fori(1, GROUPS) as g:
                    group(g, L * GROUPS + g - 1)
                group(None, L * GROUPS + GROUPS - 1)

                hold(pe, yssm_ready, 8 * L + 8)
                with pe.Fori(0, KT) as m:
                    gemm(L, T_MRG, 2 * m, 0, [four(L, B_MRG, m, 0)], x_half)
                    gemm(L, T_MRG, 2 * m, 1, [four(L, B_MRG, m, 1)], x_half)
                    gemm(L, T_MRG, 2 * m, 2, [four(L, B_MRG, m, 2), four(L, B_MRG, m, 3)],
                         lambda k, h: yssm[:, k, h * HT:(h + 1) * HT])
                    buf = claim(L, T_MRG, 2 * m, 3)
                    pe.wait_ge(wab_ld, 16 * (8 * L + m) + 16)
                    for k in range(2):
                        for h in range(2):
                            mm = nc.tensor.matmul(acc[buf][:, 512 * h:512 * h + HT],
                                                  wab[:, k, :],
                                                  oT[:, k, h * HT:(h + 1) * HT], start=k == 0, stop=k == 1)
                    mm.then_inc(acc_done, 1)
                hold(pe, mrg_done, 8 * L + 9)
                with pe.Fori(0, 2) as i:
                    for k in range(4):
                        gemm(L, T_WO, 2 * i, k, [four(L, B_WO, i, k)], lambda kk, h: merged[:, kk, h * HT:(h + 1) * HT])
                layer_norm(2 * L)
                hold(pe, x_ready, 16 * L + 24)
                for f in range(2):
                    with pe.Fori(0, 4) as i:
                        for k in range(4):
                            gemm(L, T_FFN + 24 * f, 2 * i, k, [four(L, B_FFN, 8 * f + i, k)], x_half)
                    hold(pe, hid_ready, 32 * L + 16 * f + 16)
                    with pe.Fori(0, 4) as i:
                        for k in range(2):
                            gemm(L, T_FFN + 24 * f + 16, i, k,
                                 [four(L, B_FFN, 8 * f + 4 + i, 2 * k), four(L, B_FFN, 8 * f + 4 + i, 2 * k + 1)],
                                 lambda kk, h: hid[:, kk, h * HT:(h + 1) * HT])
                layer_norm(2 * L + 1)

        @block.scalar
        def _(act):
            act.wait_ge(const_set, 3)

            def unit_done(slot_use):
                slot, use = slot_use
                act.wait_ge(w_used[slot], use + 2)

            def evac(L, base, pairs, k, slot_use, out, func, **kw):
                unit_done(slot_use)
                b = (base + k) % 2
                nc.scalar.activation(halves(out), two(acc[b]), func, **kw).then_inc(acc_free[b], 1)

            def layer_norm(n, col):
                act.wait_ge(ln_sum, n + 1)
                nc.scalar.activation(halves(mean), two(px01), ACT.Copy, scale=1.0 / D).then_inc(ln_mean, 1)
                for k in range(KT):
                    act.wait_ge(ln_c, 8 * n + k + 1)
                    act.wait_ge(ln_sqf, 8 * n + k + 1)
                    nc.scalar.activation(lsq[:, k % 2, :], xT[:, k, :], ACT.Square).then_inc(ln_sq, 1)
                act.wait_ge(ln_sqf, 8 * n + 10)
                nc.scalar.activation(halves(sdev), two(px23), ACT.Sqrt, bias=eps[:, :], scale=1.0 / D)\
                  .then_inc(ln_sd, 1)
                for k in range(KT):
                    act.wait_ge(ln_n, 8 * n + k + 1)
                    nc.scalar.activation(xT[:, k, :], xT[:, k, :], ACT.Identity, bias=lnp[:, col + 8 + k:col + 9 + k],
                                         scale=lnp[:, col + k:col + k + 1]).then_inc(x_ready, 1)

            with act.Fori(0, DEPTH) as L:
                act.wait_ge(acc_done, COUNTED * L + N_DT + 1)
                act.wait_ge(lay_ld, 80 * L + 80)
                nc.scalar.activation(halves(d_e), two(acc[0], HEADS), ACT.Abs, bias=hpar[:, 0:1])
                nc.scalar.activation(halves(d_r), two(acc[0], HEADS), ACT.Relu, bias=hpar[:, 0:1])\
                  .then_inc(acc_free[0], 1)
                act.drain()
                nc.scalar.activation(d_e, d_e, ACT.Exp, scale=-1.0)
                nc.scalar.activation(a_col[:, :], hpar[:, 1:2], ACT.Exp).then_inc(dt_exp, 1)
                act.wait_ge(dt_scan, L + 1)
                nc.scalar.activation(de_t[:, :], de_t[:, :], ACT.Exp).then_inc(de_ready, 1)
                with act.Fori(0, 3) as i:
                    for j in range(2):
                        for c in range(3):
                            k = 3 * j + c
                            su = six(L, B_QKV, i, k)
                            if c < 2:
                                act.wait_ge(rope_done, 12 * L + 4 * i + 2 * j + c + 1)
                                unit_done(su)
                                b = (T_QKV + k) % 2
                                nc.scalar.activation(halves(rraw[:, c, :]), two(acc[b]), ACT.Copy)
                                act.drain().then_inc(acc_free[b], 1)
                                act.sem_inc(rope_raw, 1)
                            else:
                                out = qkvT[:, bass.ds(12 + 2 * i + j, 1), :].rearrange("p a n -> p (a n)")
                                evac(L, T_QKV, 3 * i, k, su, out, ACT.Copy)
                act.drain()
                act.wait_ge(rope_done, 12 * L + 14)
                act.wait_ge(zeroed, L + 1)
                by_class = qkvT[:, :, 0:SEQ].rearrange("p t (n r) -> p t n r", r=RES)
                qz_h = qz.rearrange("p g (q e) n -> p (g q) e n", e=2)
                with act.Fori(0, RES) as r:
                    act.wait_ge(acc_done, COUNTED * L + N_ATT + 4 * r)
                    act.wait_ge(vr_t, 4 * L + r + 1)
                    for e in range(2):
                        rows = slice(HD * e, HD * e + HD)
                        nc.scalar.activation(qz_h[rows, :, e, :], by_class[rows, 0:6, :, bass.ds(r, 1)].squeeze(),
                                             ACT.Copy)
                    nc.scalar.activation(kr, by_class[:, 8:12, :, bass.ds(r, 1)].squeeze(), ACT.Copy)
                    nc.scalar.activation(vr, by_class[:, 14:18, :, bass.ds(r, 1)].squeeze(), ACT.Copy)
                    act.drain().then_inc(staged, 1)
                    for h in range(4):
                        act.wait_ge(s_max, 16 * L + 4 * r + h + 1)
                        nc.scalar.activation(sc[:, h % 2, :], sc[:, h % 2, :], ACT.Exp, bias=rowmax[:, h:h + 1],
                                             accum_out=rowsum[:, h:h + 1])
                        act.drain().then_inc(s_exp, 1)
                act.wait_ge(ss_max, L + 1)
                nc.scalar.activation(sc_s, sc_s, ACT.Exp, bias=rowmax[:, 0:1], accum_out=rowsum[:, 0:1])
                act.drain().then_inc(ss_exp, 1)
                act.wait_ge(att_done, L + 1)

                def group(g, s):
                    c = None if g is None else L * GROUPS + g

                    def conv_init(q):
                        nc.scalar.activation(post[:, q, :], raw[:, q, :], ACT.Identity,
                                             bias=gconv[:, 16 + q:17 + q], scale=gconv[:, 4 * q + 3:4 * q + 4])\
                          .then_inc(post_init, 1)

                    def conv_act(q):
                        act.wait_ge(conv_done, 4 * c + q + 1)
                        if q >= 2:
                            act.wait_ge(post_ready, 4 * c + q - 1)
                        nc.scalar.activation(th[:, q % 2, :], post[:, q, :], ACT.Tanh).then_inc(th_ready, 1)

                    def decay(k):
                        n = CHUNK if k < NC else TS
                        act.wait_ge(seg_ready, 5 * s + k + 1)
                        v = seg[0:n, k % 2, :, 0:n]
                        nc.scalar.activation(v, v, ACT.Exp).then_inc(e_ready, 1)

                    def tile(k):
                        if s is not None:
                            if k < 4:
                                act.wait_ge(conv_done, 4 * c - 4 + k + 1)
                            elif k == 4:
                                act.wait_ge(zs_done, s + 1)
                        evac(L, T_GRP, 3 * g, k, six(L, B_GRP, g, k), raw[:, k, :], ACT.Copy,
                             scale=1.0 if k < 4 else 0.5)

                    if s is not None:
                        act.drain()
                        nc.scalar.activation(thz, raw[:, 4:6, :], ACT.Tanh).then_inc(thz_ready, 1)
                        decay(0)
                        act.wait_ge(acb_ld, 16 * s + 16)
                        nc.scalar.activation(ea, acb, ACT.Exp).then_inc(ea_ready, 1)
                        decay(1)
                    if g is not None:
                        tile(0)
                    if s is not None:
                        decay(2)
                    if g is not None:
                        tile(1)
                    if s is not None:
                        decay(3)
                        decay(4)
                    if g is not None:
                        tile(2)
                        act.drain()
                        act.wait_ge(gp_ready, c + 1)
                    if s is not None:
                        act.wait_ge(y_evac, 2 * s + 2)
                    if g is not None:
                        conv_init(0)
                        conv_init(1)
                        conv_init(2)
                    if s is not None:
                        act.wait_ge(gated, s + 1)
                        nc.scalar.activation(sqb, yg, ACT.Square).then_inc(sq_ready, 1)
                    if g is not None:
                        conv_act(0)
                        tile(3)
                        act.drain()
                        conv_init(3)
                        conv_act(1)
                        conv_act(2)
                        tile(4)
                    if s is not None:
                        act.wait_ge(rms_sum, s + 1)
                        nc.scalar.activation(halves(rsb), px_mid, ACT.Sqrt, bias=eps[:, :], scale=1.0 / 256)\
                          .then_inc(rs_ready, 1)
                    if g is not None:
                        conv_act(3)
                        tile(5)

                group(0, None)
                with act.Fori(1, GROUPS) as g:
                    group(g, L * GROUPS + g - 1)
                group(None, L * GROUPS + GROUPS - 1)
                act.wait_ge(yssm_ready, 8 * L + 8)
                with act.Fori(0, KT) as m:
                    act.wait_ge(mrg_done, 8 * L + m + 1)
                    for k in range(2):
                        unit_done(four(L, B_MRG, m, k))
                        nc.scalar.activation(halves(gates[:, k, :]), two(acc[(T_MRG + k) % 2]), ACT.Tanh, scale=0.5)
                        act.drain().then_inc(acc_free[(T_MRG + k) % 2], 1)
                        act.sem_inc(gate_th, 1)
                layer_norm(2 * L, 0)
                for f in range(2):
                    with act.Fori(0, 4) as i:
                        for k in range(4):
                            evac(L, T_FFN + 24 * f, 2 * i, k, four(L, B_FFN, 8 * f + i, k),
                                 hid[:, bass.ds(4 * i + k, 1), :].rearrange("p a n -> p (a n)"), ACT.Relu)
                layer_norm(2 * L + 1, 16)

        @block.vector
        def _(dve):
            nc.vector.memset(ones[:, :], 1.0)
            nc.vector.memset(eps[:, :], EPS)
            nc.vector.memset(tokm[:, :, :, :], 0.0)
            dve.drain().then_inc(const_set, 3)
            dve.wait_ge(const_ld, 16 * 8)

            def layer_norm(n):
                dve.wait_ge(ln_mean, n + 1)
                for k in range(KT):
                    nc.vector.tensor_tensor(xT[:, k, :], xT[:, k, :], mean, ALU.subtract).then_inc(ln_c, 1)
                dve.wait_ge(ln_sd, n + 1)
                nc.vector.reciprocal(rstd, sdev)
                dve.drain()
                for k in range(KT):
                    nc.vector.tensor_tensor(xT[:, k, :], xT[:, k, :], rstd, ALU.mult).then_inc(ln_n, 1)

            def unit_done(slot_use):
                slot, use = slot_use
                dve.wait_ge(w_used[slot], use + 2)

            with dve.Fori(0, DEPTH) as L:
                dve.wait_ge(dt_exp, L + 1)
                nc.vector.tensor_scalar(d_z, d_e, 2.0, None, ALU.add)
                dve.drain()
                nc.vector.reciprocal(d_z, d_z)
                dve.drain()
                nc.vector.tensor_tensor(d_z, d_z, d_e, ALU.mult)
                dve.drain()
                nc.vector.tensor_tensor(d_z2, d_z, d_z, ALU.mult)
                dve.drain()
                nc.vector.tensor_scalar(d_e, d_z2, 2.0 / 17, None, ALU.mult)
                for j in range(7, 0, -1):
                    dve.drain()
                    nc.vector.scalar_tensor_tensor(d_e, d_e, 2.0 / (2 * j + 1), d_z2, ALU.add, ALU.mult)
                dve.drain()
                nc.vector.scalar_tensor_tensor(d_e, d_e, 2.0, d_z, ALU.add, ALU.mult)
                dve.drain()
                nc.vector.tensor_tensor(dt_t[:, :], d_e, d_r, ALU.add)
                dve.drain()
                nc.vector.tensor_scalar(d_z, dt_t[:, :], a_col[:, 0:1], -1.0, ALU.mult, ALU.mult)
                dve.drain()
                nc.vector.tensor_tensor_scan(ac_t[:, :], restart[:, :], d_z, 0.0, ALU.mult, ALU.add)
                dve.drain()
                for lo, a, b in ((0, NC, CHUNK), (SEQ, NB, NS)):
                    v = ac_t[:, lo:lo + a * b].rearrange("p (a b) -> p a b", a=a)
                    w = de_t[:, lo:lo + a * b].rearrange("p (a b) -> p a b", a=a)
                    end = v[:, :, b - 1:b].to_broadcast([HEADS, a, b])
                    nc.vector.tensor_tensor(w, end, v, ALU.subtract)
                dve.drain().then_inc(dt_scan, 1)
                with dve.Fori(0, 3) as i:
                    for j in range(2):
                        for c in range(2):
                            rho = 12 * L + 4 * i + 2 * j + c
                            dve.wait_ge(rope_sw, rho + 1)
                            out = qkvT[:, bass.ds(6 * c + 2 * i + j, 1), :].rearrange("p a n -> p (a n)")
                            nc.vector.tensor_tensor(halves(rtmp), two(px01), halves(sinT[:, :]), ALU.mult)\
                              .then_inc(rope_px, 1)
                            nc.vector.tensor_tensor(out, rraw[:, c, :], cosT[:, :], ALU.mult)
                            dve.drain()
                            nc.vector.tensor_tensor(out, out, rtmp, ALU.add)
                            dve.drain().then_inc(rope_done, 1)
                dve.wait_ge(tok_t, L + 1)
                per = 3 * HEADS
                nc.vector.tensor_copy(tokm[:, 0:NC, :, :].rearrange("p a b c -> p (a b c)"), X[2][:, 0:NC * per])
                nc.vector.tensor_copy(tokm[0:TS, NC, :, :].rearrange("p b c -> p (b c)"),
                                      X[2][0:TS, NC * per:(NC + 1) * per])
                dve.drain().then_inc(tok_ready, 1)
                for j in range(2):
                    dve.wait_ge(vt_t, 4 * L + j + 1)
                    nc.vector.tensor_copy(vtok[:, :, j * P:(j + 1) * P], X[j].rearrange("p (b n) -> p b n", b=NC))\
                      .then_inc(vt_done, 1)
                dve.wait_ge(vt_t, 4 * L + 3)
                nc.vector.tensor_copy(vtok_s[:, 0:512], X[3][0:TS, :]).then_inc(vt_done, 1)
                dve.wait_ge(vt_t, 4 * L + 4)
                nc.vector.tensor_copy(vtok_s[:, 512:768], X[0][0:TS, 0:256]).then_inc(vt_done, 1)
                hold(dve, mask_ld, 32 * L + 32)
                with dve.Fori(0, RES) as r:
                    dve.wait_ge(vr_t, 4 * L + r + 2)
                    nc.vector.tensor_copy(v_res.rearrange("p a n -> p (a n)"), X[2]).then_inc(vr_done, 1)

                    def softmax(h):
                        idx = 16 * L + 4 * r + h
                        b = (T_ATT + h) % 2
                        dve.wait_ge(acc_done, COUNTED * L + N_ATT + 4 * r + h + 1)
                        dve.wait_ge(pt_t, idx - 1 + 2)
                        nc.vector.scalar_tensor_tensor(
                            sc[:, h % 2, :], acc[b][:, 0:KEYS], HD ** -0.5,
                            mask[:, bass.ds(r, 1), :].rearrange("p a n -> p (a n)"), ALU.mult, ALU.add)\
                          .then_inc(acc_free[b], 1)
                        dve.drain()
                        nc.vector.tensor_reduce(rowmax[:, h:h + 1], sc[:, h % 2, :], AX_X, ALU.max, negate=True)\
                          .then_inc(s_max, 1)

                    def probs(h):
                        idx = 16 * L + 4 * r + h
                        dve.wait_ge(pt_t, idx + 3)
                        dve.wait_ge(pv_done, idx + 1)
                        nc.vector.tensor_copy(pt, px01[:, 0:KEYS]).then_inc(pt_done, 1)

                    softmax(0)
                    softmax(1)
                    probs(0)
                    softmax(2)
                    probs(1)
                    softmax(3)
                    probs(2)
                    probs(3)
                    nc.vector.reciprocal(rowinv, rowsum)
                    dve.drain()
                    dve.wait_ge(pv_done, 16 * L + 4 * r + 5)
                    nc.vector.tensor_tensor(ob.rearrange("p (h n) -> p h n", h=HG),
                                            X[3][:, 0:256].rearrange("p (h n) -> p h n", h=HG), bc(rowinv, HD),
                                            ALU.mult).then_inc(o_norm, 1)
                    dve.wait_ge(ot_t, 4 * L + r + 1)
                    nc.vector.tensor_copy(
                        oT[:, :, 0:SEQ].rearrange("p t (n r) -> p t n r", r=RES)[:, :, :, bass.ds(r, 1)].squeeze(),
                        X[2][:, 0:256].rearrange("p (t n) -> p t n", t=2)).then_inc(ot_done, 1)
                b = T_SMP % 2
                dve.wait_ge(acc_done, COUNTED * L + N_SMP + 1)
                nc.vector.scalar_tensor_tensor(sc_s, acc[b][:, 0:SKEYS], HD ** -0.5, mask_s, ALU.mult, ALU.add)\
                  .then_inc(acc_free[b], 1)
                dve.drain()
                nc.vector.tensor_reduce(rowmax[:, 0:1], sc_s, AX_X, ALU.max, negate=True).then_inc(ss_max, 1)
                dve.wait_ge(ss_exp, L + 1)
                nc.vector.reciprocal(rowinv[:, 0:1], rowsum[:, 0:1])
                dve.drain()
                nc.vector.tensor_scalar(sc_s, sc_s, rowinv[:, 0:1], None, ALU.mult).then_inc(ss_norm, 1)
                dve.wait_ge(spt_t, L + 1)
                for half in range(2):
                    out = ptz[:, half].rearrange("p k (q e n) -> p k q e n", q=4, e=2)[:, :, :, half, :]
                    src = px01[:, 0:KEYS].rearrange("p (k q e n) -> p k q e n", k=6, q=4, e=2)[:, :, :, half, :]
                    nc.vector.tensor_copy(out, src)
                nc.vector.tensor_copy(ptn, X[2][0:TS, 0:3 * P].rearrange("p (g n) -> p g n", g=3))
                dve.drain().then_inc(spt_done, 1)
                dve.wait_ge(c_used, 8 * L + 8)
                nc.vector.tensor_copy(ob, X[3][:, 0:256]).then_inc(so_copy, 1)
                dve.wait_ge(so_t, L + 1)
                for h in range(HG):
                    rows = slice(HD * (h % 2), HD * (h % 2) + HD)
                    src = X[2][rows, (h // 2) * P:(h // 2 + 1) * P].rearrange("p (b h t) -> p b h t", b=NB, h=HG)
                    nc.vector.tensor_copy(oT[rows, h // 2, SEQ:T].rearrange("p (b t) -> p b t", b=NB), src[:, :, h, :])
                dve.drain().then_inc(att_done, 1)

                def group(g, gs):
                    c = None if g is None else L * GROUPS + g
                    s = None if gs is None else L * GROUPS + gs

                    def conv(q):
                        dve.wait_ge(post_init, 4 * c + q + 1)
                        dve.wait_ge(spad_ready, 4 * c + q + 1)
                        u = post[:, q, :]
                        us = u[:, SEQ:T].rearrange("p (b t) -> p b t", b=NB)
                        pad = spad[:, q].rearrange("p (b t) -> p b t", b=NB)
                        for tap in (2, 1, 0):
                            lag = CW - 1 - tap
                            w = gconv[:, 4 * q + tap:4 * q + tap + 1]
                            nc.vector.scalar_tensor_tensor(u[:, lag:SEQ], raw[:, q, 0:SEQ - lag], w, u[:, lag:SEQ],
                                                           ALU.mult, ALU.add)
                            nc.vector.scalar_tensor_tensor(us, pad[:, :, tap:tap + NS], w, us, ALU.mult, ALU.add)
                            if tap:
                                dve.drain()
                        dve.drain().then_inc(conv_done, 1)

                    def silu(q):
                        dve.wait_ge(th_ready, 4 * c + q + 1)
                        nc.vector.scalar_tensor_tensor(post[:, q, :], th[:, q % 2, :], 1.0, post[:, q, :],
                                                       ALU.add, ALU.mult).then_inc(post_ready, 1)

                    def exponents(k):
                        n = CHUNK if k < NC else TS
                        for hh in range(HG):
                            nc.vector.tensor_scalar(seg[0:n, k % 2, hh, 0:n], acb[0:n, hh, k * CHUNK:k * CHUNK + n],
                                                    gt[0:n, k, 1, hh:hh + 1], 0.0, ALU.subtract, ALU.min)
                        dve.drain().then_inc(seg_ready, 1)

                    def chunk(k):
                        n = CHUNK if k < NC else TS
                        dve.wait_ge(t_done, 5 * s + k + 1)
                        nc.vector.tensor_tensor(xdt[0:n, :].rearrange("p (h d) -> p h d", h=HG),
                                                X[0][0:n, 0:256].rearrange("p (h d) -> p h d", h=HG),
                                                bc(gt[0:n, k, 0, :], HD), ALU.mult)
                        nc.vector.tensor_copy(btok[0:n, :], X[0][0:n, 256:384])
                        nc.vector.tensor_tensor(cbm[0:n, 0:n], X[0][0:n, 384:384 + n],
                                                (tri if k < NC else tri_s)[0:n, 0:n], ALU.mult)
                        dve.drain().then_inc(x0_free, 1)
                        dve.wait_ge(e_ready, 5 * s + k + 1)
                        nc.vector.tensor_tensor(mdec[0:n, :, 0:n], seg[0:n, k % 2, :, 0:n],
                                                cbm[0:n, 0:n].unsqueeze(1).to_broadcast([n, HG, n]), ALU.mult)\
                          .then_inc(m_ready, 1)
                        if k + 2 <= NC:
                            dve.drain()
                            exponents(k + 2)
                        if k == NC:
                            return
                        hv = hst.rearrange("p (h d) -> p h d", h=HG)
                        dve.wait_ge(y_done, 5 * s + k + 1)
                        if k > 0:
                            last = (k + 1) * CHUNK - 1
                            nc.vector.tensor_tensor(hv, hv, ea[:, :, last:last + 1].to_broadcast([P, HG, HD]), ALU.mult)
                            dve.drain()
                            nc.vector.tensor_tensor(hst, hst, X[3][:, 0:256], ALU.add).then_inc(h_ready, 1)
                        else:
                            dve.wait_ge(h_free, s + 1)
                            nc.vector.tensor_copy(hst, X[3][:, 0:256]).then_inc(h_ready, 1)

                    def add_states(j):
                        dve.wait_ge(ns_done, 4 * s + j + 1)
                        v = st[:, 2 * j:2 * j + 2, :].rearrange("p b n -> p (b n)")
                        nc.vector.tensor_tensor(v, v, X[3 * (j % 2)], ALU.add).then_inc(ns_add, 1)

                    dve.drain()
                    if g is not None:
                        nc.vector.tensor_scalar(gconv[:, :], par[:, bass.ds(g, 1), 0:20].rearrange("p a n -> p (a n)"),
                                                0.5, None, ALU.mult)
                        dve.drain().then_inc(gp_ready, 1)
                    if s is not None:
                        nc.vector.tensor_copy(gp[:, :], par[:, bass.ds(gs, 1), 20:NGP].rearrange("p a n -> p (a n)"))
                        nc.vector.tensor_copy(gt[:, :, :, :].rearrange("p a b c -> p (a b) c"),
                                              tokm[:, :, :, bass.ds(gs * HG, HG)].rearrange("p a b c -> p (a b) c"))
                        dve.drain()
                        dve.wait_ge(acb_ld, 16 * s + 16)
                        exponents(0)
                        exponents(1)
                        dve.wait_ge(ea_ready, s + 1)
                        for k in range(NC + 1):
                            chunk(k)
                            if k == 0:
                                dve.wait_ge(thz_ready, s + 1)
                                nc.vector.scalar_tensor_tensor(zs, thz, 1.0, raw[:, 4:6, :], ALU.add, ALU.mult)\
                                  .then_inc(zs_done, 1)
                            if k == NC - 1:
                                for j in range(2):
                                    ins = nc.vector.scalar_tensor_tensor(yg[:, j, 0:SEQ], post[:, 2 + j, 0:SEQ],
                                                                         gp[:, j:j + 1], X[1 + j], ALU.mult, ALU.add)
                                ins.then_inc(y_evac, 1)
                        dve.wait_ge(y_done, 5 * s + 5)
                        for j in range(2):
                            ins = nc.vector.scalar_tensor_tensor(yg[:, j, SEQ:T], post[:, 2 + j, SEQ:T], gp[:, j:j + 1],
                                                                 X[3][:, 256 + TS * j:256 + TS * (j + 1)],
                                                                 ALU.mult, ALU.add)
                        ins.then_inc(y_evac, 1)
                        dve.drain()
                        nc.vector.tensor_tensor(yg, yg, zs, ALU.mult).then_inc(gated, 1)
                    if g is not None:
                        conv(0)
                        conv(1)
                        silu(0)
                    if s is not None:
                        dve.wait_ge(st_dec, s + 1)
                        add_states(0)
                        add_states(1)
                    if g is not None:
                        conv(2)
                        silu(1)
                    if s is not None:
                        add_states(2)
                        add_states(3)
                    if g is not None:
                        conv(3)
                        silu(2)
                    if s is not None:
                        dve.wait_ge(rs_ready, s + 1)
                        nc.vector.reciprocal(rsb, rsb)
                    if g is not None:
                        silu(3)
                    if s is not None:
                        dve.drain()
                        for j in range(2):
                            ins = nc.vector.scalar_tensor_tensor(
                                yssm[:, bass.ds(2 * gs + j, 1), :].rearrange("p a n -> p (a n)"), yg[:, j, :],
                                gp[:, 2 + j:3 + j], rsb, ALU.mult, ALU.mult)
                        ins.then_inc(yssm_ready, 1)

                group(0, None)
                with dve.Fori(1, GROUPS) as g:
                    group(g, g - 1)
                group(None, GROUPS - 1)

                with dve.Fori(0, KT) as m:
                    dve.drain()
                    for k in range(2):
                        dve.wait_ge(gate_th, 16 * L + 2 * m + k + 1)
                        nc.vector.tensor_scalar(gates[:, k, :], gates[:, k, :], 0.5, 0.5, ALU.mult, ALU.add)
                    dve.drain()
                    unit_done(four(L, B_MRG, m, 3))
                    b = (T_MRG + 2) % 2
                    nc.vector.tensor_tensor(halves(prod[:, 0, :]), two(acc[b]), halves(gates[:, 0, :]), ALU.mult)\
                      .then_inc(acc_free[b], 1)
                    dve.wait_ge(acc_done, COUNTED * L + N_MRG + m + 1)
                    nc.vector.tensor_tensor(halves(prod[:, 1, :]), two(acc[1 - b]), halves(gates[:, 1, :]), ALU.mult)\
                      .then_inc(acc_free[1 - b], 1)
                    dve.drain()
                    nc.vector.tensor_tensor(merged[:, bass.ds(m, 1), :].rearrange("p a n -> p (a n)"), prod[:, 0, :],
                                            prod[:, 1, :], ALU.add).then_inc(mrg_done, 1)
                with dve.Fori(0, 2) as i:
                    for k in range(4):
                        unit_done(four(L, B_WO, i, k))
                        b = (T_WO + k) % 2
                        v = halves(xT[:, bass.ds(4 * i + k, 1), :].rearrange("p a n -> p (a n)"))
                        nc.vector.scalar_tensor_tensor(v, v, ALPHA, two(acc[b]), ALU.mult, ALU.add)
                        dve.drain().then_inc(acc_free[b], 1)
                        dve.sem_inc(ln_x, 1)
                layer_norm(2 * L)
                for f in range(2):
                    with dve.Fori(0, 4) as i:
                        for k in range(4):
                            dve.wait_ge(acc_free[(T_FFN + k) % 2], read_of(L, T_FFN + 24 * f, 2 * i, k))
                            v = hid[:, bass.ds(4 * i + k, 1), :].rearrange("p a n -> p (a n)")
                            nc.vector.tensor_tensor(v, v, v, ALU.mult).then_inc(hid_ready, 1)
                    with dve.Fori(0, 4) as i:
                        for k in range(2):
                            unit_done(four(L, B_FFN, 8 * f + 4 + i, 2 * k + 1))
                            b = (T_FFN + k) % 2
                            x = halves(xT[:, bass.ds(2 * i + k, 1), :].rearrange("p a n -> p (a n)"))
                            p = halves(part[:, bass.ds(2 * i + k, 1), :].rearrange("p a n -> p (a n)"))
                            if f == 0:
                                nc.vector.scalar_tensor_tensor(p, x, ALPHA, two(acc[b]), ALU.mult, ALU.add)\
                                  .then_inc(acc_free[b], 1)
                            else:
                                nc.vector.tensor_tensor(x, p, two(acc[b]), ALU.add)
                                dve.drain().then_inc(acc_free[b], 1)
                                dve.sem_inc(ln_x, 1)
                layer_norm(2 * L + 1)

        @block.gpsimd
        def _(pool):
            for s_, n in ([(w, 1) for w in w_used] + [(a, 1) for a in acc_free] +
                          [(rope_px, 1), (rope_done, 2), (vr_t, 1), (pt_t, 2), (pt_done, 1), (pv_done, 1), (o_norm, 1),
                           (ot_done, 1), (mrg_done, 1), (ln_sqf, 2), (h_free, 1)]):
                pool.sem_inc(s_, n)

            def row(ap, i, pat):
                return ap[bass.ds(i, 1)].rearrange(pat)

            with pool.Fori(0, DEPTH) as L:
                hold(pool, x_ready, 16 * L + 16)
                for t, name in ((wdt, "wdt"), (par, "par"), (cst, "cst")):
                    pool.dma_start(t[:, :, :], row(A[name], L, "o p a b -> (o p) a b")).then_inc(lay_ld, 16)
                for t, name in ((lnp, "lnp"), (hpar, "hpar")):
                    pool.dma_start(t[:, :], row(A[name], L, "o p a -> (o p) a")).then_inc(lay_ld, 16)
                pool.dma_start(mask.bitcast(U16), A["mask"]).then_inc(mask_ld, 16)
                pool.dma_start(mask_s.bitcast(U16), A["mask_s"]).then_inc(mask_ld, 16)
                pool.memset(qz, 0.0)
                pool.memset(qzs, 0.0)
                pool.memset(ptz, 0.0)
                pool.drain().then_inc(zeroed, 1)
                for b in range(4):
                    pool.dma_start(cring[:, b, :], row(A["kc"], L * NB + b, "o p n -> (o p) n")).then_inc(c_loaded[b], 16)
                hold(pool, dt_scan, L + 1)
                pool.dma_start(A["ac"], ac_t[:, :]).then_inc(ac_stored, 16)
                hold(pool, rope_done, 12 * L + 14)
                for e in range(2):
                    rows = slice(HD * e, HD * e + HD)
                    for p in range(2):
                        for half in range(2):
                            at = half * 16 + (2 * p + e) * NS
                            out = qzs[rows, :, p].rearrange("d g (q w) n -> d g q w n", w=2)[:, :, :, half, at:at + NS]
                            src = qkvT[rows, 0:6, SEQ:T].rearrange("d (g p) (q w t) -> d g p q w t", p=2, q=4, w=2)[
                                :, :, p, :, half, :]
                            pool.tensor_copy(out, src)
                pool.drain().then_inc(qzs_ready, 1)
                hold(pool, acc_free[0], read_of(L, T_QKV, 6, 5))
                pool.dma_start(row(A["kv"], L, "o p t n -> (o p) t n"), qkvT[:, 6:18, :]).then_inc(kv_st, 16)
                for b in range(4, 8):
                    hold(pool, c_used, 8 * L + b // 2 - 1)
                    pool.dma_start(cring[:, b % 4, :], row(A["kc"], L * NB + b, "o p n -> (o p) n"))\
                        .then_inc(c_loaded[b % 4], 16)
                for b in range(8):
                    hold(pool, c_used, 8 * L + b // 2 + 3)
                    pool.dma_start(cring[:, b % 4, :], row(A["vc"], L * NB + b, "o p n -> (o p) n"))\
                        .then_inc(c_loaded[b % 4], 16)
                hold(pool, kv_st, 16 * L + 16)
                hold(pool, att_done, L + 1)

                def load_decay(gi, s):
                    pool.dma_start(acb, A["ac"][bass.ds(gi * HG, HG), :].partition_broadcast(P)).then_inc(acb_ld, 16)

                def load_state(gi, s):
                    pool.dma_start(st, row(A["st"], s, "o p b n -> (o p) b n")).then_inc(st_ld, 16)

                hold(pool, ac_stored, 16 * L + 16)
                load_decay(0, L * GROUPS)
                load_state(0, L * GROUPS)

                def pad_of(g, q):
                    c = L * GROUPS + g
                    hold(pool, acc_free[q % 2], read_of(L, T_GRP, 3 * g, q))
                    pad = spad[:, q].rearrange("p (b t) -> p b t", b=NB)
                    pool.tensor_copy(pad[:, :, CW - 1:], raw[:, q, SEQ:T].rearrange("p (b t) -> p b t", b=NB))
                    pool.tensor_copy(pad[:, :, 0:CW - 1], cst[:, bass.ds(4 * g + q, 1), :].rearrange(
                        "p a (b t) -> p (a b) t", b=NB))
                    pool.tensor_copy(cout[:, q, :], raw[:, q, T - 35:T])
                    pool.drain().then_inc(spad_ready, 1)
                    if q == 3:
                        pool.dma_start(row(A["cout"], c, "o p q n -> (o p) q n"), cout).then_inc(cout_st, 16)

                def side(s, k):
                    n = CHUNK if k < NC else TS
                    hold(pool, x0_free, 5 * s + k + 1)
                    cols = slice(k * CHUNK, k * CHUNK + n)

                    def weigh_x():
                        pool.tensor_tensor(xde[0:n, :].rearrange("p (h d) -> p h d", h=HG),
                                           xdt[0:n, :].rearrange("p (h d) -> p h d", h=HG), bc(gt[0:n, k, 2, :], HD),
                                           ALU.mult)

                    if k < NC:
                        weigh_x()
                    if k > 0:
                        pool.tensor_tensor(cea[:, :, 0:n], ea[:, :, cols], post[:, 1:2, cols].to_broadcast([P, HG, n]),
                                           ALU.mult)
                    pool.drain().then_inc(pool_step, 1)
                    if k == NC:
                        weigh_x()
                        pool.tensor_tensor(bm, bc(bmask[:, :], P),
                                           btok[0:TS, :].unsqueeze(1).to_broadcast([TS, NB, P]), ALU.mult)
                        pool.drain().then_inc(bm_ready, 1)

                def group(g, s):
                    if s is not None:
                        side(s, 0)
                        side(s, 1)
                    if g is not None:
                        pad_of(g, 0)
                    if s is not None:
                        side(s, 2)
                        side(s, 3)
                    if g is not None:
                        pad_of(g, 1)
                    if s is not None:
                        side(s, 4)
                        hold(pool, h_ready, 4 * s + 4)
                        pool.dma_start(row(A["hout"], s, "o p n -> (o p) n"), hst).then_inc(h_st, 16)
                        hold(pool, y_done, 5 * s + 5)
                        ends = ea[:, :, SEQ + NS - 1:T:NS].rearrange("p h b -> p b h")
                        for b in range(NB):
                            v = st[:, b, :].rearrange("p (h d) -> p h d", h=HG)
                            pool.tensor_tensor(v, v, bc(ends[:, b, :], HD), ALU.mult)
                        pool.drain().then_inc(st_dec, 1)
                    if g is not None:
                        if s is not None:
                            load_decay(g, s + 1)
                        pad_of(g, 2)
                        pad_of(g, 3)
                    if s is not None:
                        hold(pool, ns_add, 4 * s + 4)
                        pool.dma_start(row(A["stout"], s, "o p b n -> (o p) b n"), st).then_inc(st_st, 16)
                        hold(pool, h_st, 16 * s + 16)
                        pool.sem_inc(h_free, 1)
                        hold(pool, st_st, 16 * s + 16)
                    if g is not None:
                        if s is not None:
                            load_state(g, s + 1)
                        hold(pool, cout_st, 16 * (L * GROUPS + g) + 16)

                group(0, None)
                with pool.Fori(1, GROUPS) as g:
                    group(g, L * GROUPS + g - 1)
                group(None, L * GROUPS + GROUPS - 1)
                hold(pool, yssm_ready, 8 * L + 8)
                with pool.Fori(0, KT) as m:
                    hold(pool, mrg_done, 8 * L + m + 1)
                    pool.dma_start(wab, row(A["wab"], L * KT + m, "o p k n -> (o p) k n")).then_inc(wab_ld, 16)
    return nc


def rotary_tables():
    half = ROPE // 2
    inv = np.power(np.float32(THETA), -np.arange(half, dtype=np.float32) / half).astype(np.float32)
    pos = np.concatenate([np.arange(SEQ), np.tile(PAST + np.arange(NS), NB)]).astype(np.float32)
    ang = (pos[:, None] * inv[None, :]).astype(np.float32)
    cos, sin = np.ones((P, T), np.float32), np.zeros((P, T), np.float32)
    swap = np.zeros((P, P), np.float32)
    for head in range(2):
        for d in range(half):
            a, b = 64 * head + d, 64 * head + half + d
            cos[a] = cos[b] = np.cos(ang[:, d])
            sin[a] = sin[b] = np.sin(ang[:, d])
            swap[b, a], swap[a, b] = -1.0, 1.0
    return cos, sin, swap


def attention_masks():
    m = np.full((P, RES, KEYS), NEG, np.float32)
    i = np.arange(P)[:, None]
    for r in range(RES):
        q, j = RES * i + r, np.arange(SEQ)[None, :]
        m[:, r, 0:SEQ][(q >= j) & (q - j <= 128)] = 0
        j = np.arange(P)[None, :]
        m[:, r, SEQ:SEQ + P][i >= j] = 0
        m[:, r, SEQ + P:KEYS][(i >= j) & ((i - j) % 4 == 0)] = 0
    s = np.full((NB, HG, NS, SKEYS), NEG, np.float32)
    for b in range(NB):
        for t in range(NS):
            s[b, :, t, 0:SEQ][:, np.arange(SEQ) % 4 == t] = 0
            s[b, :, t, SEQ:SEQ + P][:, np.arange(P) >= t] = 0
            s[b, :, t, SEQ + P:KEYS][:, np.arange(P) % 4 == t] = 0
            s[b, :, t, KEYS + NS * b:KEYS + NS * b + t + 1] = 0
            for g in (1, 2):
                s[b, :, t, KEYS + TS * g + NS * b + t] = 0
    return tuple((a.view(np.uint32) >> 16).astype(np.uint16) for a in (m, s.reshape(P, SKEYS)))


def kernel(**inputs):
    import concourse.bacc as bacc
    from concourse.bass_utils import run_bass_kernel_spmd

    i = {k: np.asarray(v) for k, v in inputs.items()}
    f32 = np.float32

    def tiles(w):
        k, n = w.shape
        return w.reshape(k // D, KT, P, n // P, P).transpose(3, 0, 2, 1, 4).reshape(n // P, k // D, P, KT * P)

    units = np.empty((DEPTH, UNITS, P, KT * P), f32)
    for l in range(DEPTH):
        w = i["w_in"][l]
        q, k, v = (tiles(w[:, o:o + AW])[:, 0] for o in (OFF_Q, OFF_K, OFF_V))
        z, xs = tiles(w[:, 0:D_IN])[:, 0], tiles(w[:, OFF_XBC:OFF_XBC + D_IN])[:, 0]
        bb = tiles(w[:, OFF_XBC + D_IN:OFF_XBC + D_IN + D])[:, 0]
        cc = tiles(w[:, OFF_XBC + D_IN + D:OFF_DT])[:, 0]
        gs, ga = tiles(w[:, OFF_G:OFF_G + D])[:, 0], tiles(w[:, OFF_G + D:])[:, 0]
        br = tiles(i["w_ssm_br"][l])
        u = [x for j in range(6) for x in (q[j], k[j], v[j])]
        u += [x for g in range(GROUPS) for x in (bb[g], cc[g], xs[2 * g], xs[2 * g + 1], z[2 * g], z[2 * g + 1])]
        u += [x for m in range(KT) for x in (gs[m], ga[m], br[m, 0], br[m, 1])]
        u += list(tiles(i["w_o"][l])[:, 0])
        up, down = tiles(i["w_up"][l])[:, 0], tiles(i["w_down"][l])
        for f in range(2):
            u += list(up[FT * f:FT * (f + 1)])
            u += [x for m in range(KT) for x in (down[m, 2 * f], down[m, 2 * f + 1])]
        for n, x in enumerate(u):
            units[l, n] = x

    def cols(v):
        return v.reshape(DEPTH, -1, P).transpose(0, 2, 1)

    conv_cols = np.concatenate([i["conv_w"], i["conv_b"][:, None]], 1)
    conv_cols = conv_cols.reshape(DEPTH, CW + 1, CONV // P, P).transpose(0, 3, 2, 1)
    skip = cols(np.repeat(i["d_skip"], HD, axis=1))
    gain = cols(i["ssm_norm_g"])
    order = [(16 + g, 24 + g, 2 * g, 2 * g + 1) for g in range(GROUPS)]
    par = np.empty((DEPTH, P, GROUPS, NGP), f32)
    for g, t in enumerate(order):
        par[:, :, g, 0:16] = conv_cols[:, :, list(t), 0:CW].reshape(DEPTH, P, 16)
        par[:, :, g, 16:20] = conv_cols[:, :, list(t), CW]
        par[:, :, g, 20:22] = skip[:, :, 2 * g:2 * g + 2]
        par[:, :, g, 22:24] = gain[:, :, 2 * g:2 * g + 2]
    flat = [t for ts in order for t in ts]
    cst = i["state_conv"].reshape(DEPTH, NB, CW - 1, CONV // P, P).transpose(0, 4, 3, 1, 2)[:, :, flat]
    kv128, kv512, kv2048 = (i[n] for n in ("cache_kv_w128", "cache_kv_w512", "cache_kv_w2048"))
    kv2048 = kv2048.reshape(DEPTH, NB, PAST // 16, 16, 2, HG, HD)[:, :, :, 0:4].reshape(DEPTH, NB, P, 2, HG, HD)
    cache = np.concatenate([kv512, kv128, kv2048], axis=2)
    kc = cache[:, :, :, 0].reshape(DEPTH, NB, KEYS, 2, P).transpose(0, 1, 4, 3, 2).reshape(DEPTH * NB, P, 2 * KEYS)
    vc = cache[:, :, :, 1].reshape(DEPTH, NB, 6, P, 256).transpose(0, 1, 3, 2, 4).reshape(DEPTH * NB, P, 6 * 256)
    st = i["state_ssm"].reshape(DEPTH, NB, GROUPS, 256, NST).transpose(0, 2, 4, 1, 3).reshape(DEPTH * GROUPS, P, NB, 256)
    x0 = np.concatenate([i["x_prompt"].reshape(SEQ, D), i["x_sample"].reshape(TS, D)])
    x0 = x0.reshape(T, KT, P).transpose(2, 1, 0)
    wdt = i["w_in"][:, :, OFF_DT:OFF_Q].reshape(DEPTH, KT, P, HEADS).transpose(0, 2, 1, 3)
    wab = i["w_attn_br"].reshape(DEPTH, 2, P, KT, P).transpose(0, 3, 2, 1, 4).reshape(DEPTH * KT, P, 2, P)
    lnp = np.concatenate([cols(i[n]) for n in ("ln1_g", "ln1_b", "ln2_g", "ln2_b")], axis=2)
    hpar = np.stack([i["dt_bias"], i["a_log"]], axis=2)
    cos, sin, swap = rotary_tables()
    mask, mask_s = attention_masks()
    tok = np.arange(TS)
    restart = np.ones((HEADS, T), f32)
    restart[:, 0:SEQ:CHUNK] = 0
    restart[:, SEQ:T:NS] = 0
    arrays = {
        "x0": x0, "wst": units.reshape(DEPTH * UNITS, P, KT * P), "wdt": wdt, "wab": wab, "par": par, "lnp": lnp,
        "hpar": hpar, "cst": cst.reshape(DEPTH, P, 4 * GROUPS, NB * (CW - 1)), "kc": kc, "vc": vc, "st": st,
        "ident": np.eye(P, dtype=f32), "swap": swap, "cos": cos, "sin": sin,
        "tri": np.triu(np.ones((P, P), f32)),
        "tri_s": ((tok[:, None] // NS == tok[None, :] // NS) & (tok[:, None] <= tok[None, :])).astype(f32),
        "bmask": (tok[:, None] // NS == np.arange(NB)[None, :]).astype(f32), "restart": restart,
        "mask": mask.reshape(P, RES, KEYS), "mask_s": mask_s,
    }
    outs = {"y": (P, KT, T), "kv": (DEPTH, P, 12, T), "cout": (DEPTH * GROUPS, P, 4, 35),
            "hout": (DEPTH * GROUPS, P, 256), "stout": (DEPTH * GROUPS, P, NB, 256)}
    nc = bacc.Bacc("TRN2", target_bir_lowering=False, num_devices=1)
    feed, A = {}, {}
    for name, a in arrays.items():
        feed[f"in_{name}"] = np.ascontiguousarray(a)
        A[name] = nc.dram_tensor(f"in_{name}", a.shape, mybir.dt.from_np(a.dtype), kind="ExternalInput").ap()
    for name, shape in outs.items():
        A[name] = nc.dram_tensor(f"out_{name}", shape, F32, kind="ExternalOutput").ap()
    A["ac"] = nc.dram_tensor("scratch_ac", (HEADS, T), F32, kind="Internal").ap()
    build(nc, A)
    r = run_bass_kernel_spmd(nc, [feed], core_ids=[0]).results[0]
    y, kv, cout, hout, stout = (np.asarray(r[f"out_{n}"]) for n in outs)

    y = y.transpose(2, 1, 0).reshape(T, D)
    kv = kv.reshape(DEPTH, P, 2, 3, 2, T).transpose(3, 0, 5, 2, 4, 1)
    kv = kv.reshape(3, DEPTH, T, 2, HG, HD)
    kv_p = [kv[j, :, SEQ - min(w, SEQ):SEQ].reshape(DEPTH, 1, min(w, SEQ), 2, HG, HD) for j, (w, _) in enumerate(WINDOWS)]
    kv_s = [kv[j, :, SEQ:T].reshape(DEPTH, NB, NS, 2, HG, HD) for j in range(3)]
    cout = cout.reshape(DEPTH, GROUPS, P, 4, 35).transpose(0, 4, 1, 3, 2).reshape(DEPTH, 35, 4 * GROUPS, P)
    conv = np.empty((DEPTH, 35, CONV // P, P), f32)
    conv[:, :, flat] = cout
    conv = conv.reshape(DEPTH, 35, CONV)
    conv_s = conv[:, 3:].reshape(DEPTH, NB, NS, CONV)[:, :, 1:]
    ssm_p = hout.reshape(DEPTH, 1, GROUPS, P, HG, HD).transpose(0, 1, 2, 4, 5, 3).reshape(DEPTH, 1, HEADS, HD, NST)
    ssm_s = stout.reshape(DEPTH, GROUPS, P, NB, HG, HD).transpose(0, 3, 1, 4, 5, 2).reshape(DEPTH, NB, HEADS, HD, NST)
    return (y[0:SEQ].reshape(1, SEQ, D), y[SEQ:T].reshape(NB, NS, D), *kv_p, conv[:, 0:3].reshape(DEPTH, 1, 3, CONV),
            np.ascontiguousarray(ssm_p), *kv_s, np.ascontiguousarray(conv_s), np.ascontiguousarray(ssm_s))
```

```python
from contextlib import ExitStack

import numpy as np

import concourse.bass as bass
from concourse import mybir

F32 = mybir.dt.float32
F32R = mybir.dt.float32r
BF16 = mybir.dt.bfloat16
U16 = mybir.dt.uint16
ALU = mybir.AluOpType
ACT = mybir.ActivationFunctionType
AX_X = mybir.AxisListType.X

P = 128
DEPTH, D = 2, 1024
SEQ, NB, NS = 512, 8, 4
TS = NB * NS
T = SEQ + TS
HT = T // 2
KT = D // P
HEADS, GROUPS, HD, NST = 32, 8, 64, 128
HG = HEADS // GROUPS
CHUNK = 128
NC = SEQ // CHUNK
CW = 4
REG = 23840
D_IN = HEADS * HD
CONV = D_IN + 2 * GROUPS * NST
AW = 768
OFF_XBC, OFF_DT = D_IN, D_IN + CONV
OFF_Q = OFF_DT + HEADS
OFF_K, OFF_V, OFF_G = OFF_Q + AW, OFF_Q + 2 * AW, OFF_Q + 3 * AW
DFF = 4 * D
FT = DFF // P // 2
ALPHA = (2 * DEPTH) ** 0.25
EPS = 1e-5
PAST = 512
WINDOWS = ((128, 1), (512, 4), (2048, 16))
ROPE, THETA = 16, 500000.0
RES = 4
NEG = -1e30
KEYS = SEQ + 2 * P
SKEYS = KEYS + 3 * TS

SLOTS = 4
U_QKV, U_GRP, U_MRG, U_WO, U_FFN, UNITS = 0, 18, 66, 98, 106, 170
SLOT_USES = tuple(len(range(s, UNITS, SLOTS)) for s in range(SLOTS))
AHEAD = 3

T_DT, T_QKV, T_ATT, T_SMP, T_GRP, T_MRG, T_WO, T_FFN, TILES = 0, 1, 19, 35, 36, 84, 116, 124, 172
N_DT, N_ATT, N_SMP, N_MRG, COUNTED = 0, 1, 17, 18, 26

SCAN_AT = (3, 6, 8, 10, 13)
NEW_AT = (15, 17)
RMS_AT = 19
SAMPLE_K_AT = (0, 1, 2, 3)
SAMPLE_TURN_AT = 7
SAMPLE_V_AT = (9, 10, 13, 14)
SAMPLE_OUT_AT = 16

NGP = 4 * CW + 4 + 2 + 2
HP_N = 32


def unit(L, u, rounds=0):
    return u % SLOTS, L * SLOT_USES[u % SLOTS] + u // SLOTS + rounds


def build(nc, A):
    with ExitStack() as ctx:
        def sb(name, shape, dt=F32):
            return ctx.enter_context(nc.sbuf_tensor(name, shape, dt))

        def sem(name):
            return ctx.enter_context(nc.semaphore(name))

        def twins(name, shape):
            with nc.sbuf_tensor(name, shape, F32) as whole:
                pass
            return whole, sb(name + "_parts", shape, F32R)

        class Region:

            def __init__(self, name, words):
                self.t, self.split = twins(name, [P, words])
                self.words, self.at, self.high = words, 0, 0

            def take(self, *dims, parts=P, split=False):
                n = int(np.prod(dims))
                v = (self.split if split else self.t)[0:parts, self.at:self.at + n]
                self.at += n
                assert self.at <= self.words, (self.at, self.words)
                self.high = max(self.high, self.at)
                if len(dims) == 2:
                    v = v.rearrange("p (a b) -> p a b", a=dims[0])
                if len(dims) == 3:
                    v = v.rearrange("p (a b c) -> p a b c", a=dims[0], b=dims[1])
                if len(dims) == 4:
                    v = v.rearrange("p (a b c d) -> p a b c d", a=dims[0], b=dims[1], c=dims[2])
                return v

            def restart(self, at=0):
                self.at = at

        xhi = sb("xhi", [P, KT, T], F32R)
        xlo = sb("xlo", [P, KT, T], F32R)
        whole, wlo = twins("wring", [P, SLOTS, KT * P])
        whi = sb("whi", [P, SLOTS, KT * P], F32R)
        oT = sb("oT", [P, 2, T])
        ident = sb("ident", [P, P])
        ones = sb("ones", [P, P])
        swap = sb("swap", [P, P])
        tri = sb("tri", [P, P])
        tri_s = sb("tri_s", [TS, TS])
        bmask = sb("bmask", [TS, NB])
        wdt, wdt_lo = twins("wdt", [P, KT, HEADS])
        wdt_hi = sb("wdt_hi", [P, KT, HEADS], F32R)
        par = sb("par", [P, GROUPS, NGP])
        lnp = sb("lnp", [P, HP_N])
        hpar = sb("hpar", [HEADS, 2])
        cst = sb("cst", [P, 4 * GROUPS, NB * (CW - 1)])
        tokm = sb("tokm", [P, NC + 1, 3, HEADS])
        gp = sb("gp", [P, 2])
        gconv = sb("gconv", [P, 20])
        gt = sb("gt", [P, NC + 1, 3, HG])
        eps = sb("eps", [P, 1])
        warm = sb("warm", [P, 1])
        a_col = sb("a_col", [HEADS, 1])

        big = Region("big", D_IN // P * T)
        yssm = big.take(D_IN // P, T)
        big.restart()
        ylo = big.take(D_IN // P, T, split=True)
        hlo = ylo
        big.restart()
        d_e, d_r, d_z, d_z2 = (big.take(T, parts=HEADS) for _ in range(4))
        dtv = [big.take(T, parts=HEADS) for _ in range(3)]
        dt_t, ac_t, de_t = dtv
        restarts = big.take(T, parts=HEADS)
        cosT, sinT = big.take(T), big.take(T)
        big.restart()
        ptz = big.take(2, 6, P)
        cring = big.take(4, 12 * P)
        big.restart()

        reg = Region("region", REG)
        qkvT = reg.take(18, T)
        rraw = reg.take(2, T)
        rtmp = reg.take(T)
        vtok = reg.take(NC, 256)
        vtok_s = reg.take(AW, parts=TS)
        mask = reg.take(RES, KEYS // 2).bitcast(BF16)
        mask_s = reg.take(SKEYS // 2).bitcast(BF16)
        after_masks = reg.at
        qz = reg.take(3, HG, P)
        kr = reg.take(4, P)
        vr = reg.take(4, P)
        v_res = reg.take(4, P)
        sc = reg.take(2, KEYS)
        pt = reg.take(KEYS)
        rowmax = reg.take(HG)
        rowsum = reg.take(2, HG)
        rowinv = reg.take(HG)
        ob = reg.take(256)
        qzs = reg.take(3, 2, NB, 32)
        sc_s = reg.take(SKEYS)
        ptn = reg.take(3, P, parts=TS)
        reg.restart()
        st = reg.take(NB, 256)
        hst = reg.take(256)
        cout = reg.take(4, 35)
        after_stores = reg.at
        post = reg.take(4, T)
        th = reg.take(2, T)
        thz = reg.take(2, T)
        zs = reg.take(2, T)
        acb = reg.take(HG, T)
        ea = reg.take(HG, T)
        seg = reg.take(2, HG, P)
        mdec = reg.take(HG, P)
        cea = reg.take(HG, P)
        xdt = reg.take(256)
        xde = reg.take(256)
        btok = reg.take(P)
        cbm = reg.take(P)
        assert reg.at <= after_masks
        reg.restart(after_masks)
        raw = reg.take(6, T)
        bm = reg.take(NB, P, parts=TS)
        yg = reg.take(2, T)
        sqb = reg.take(2, T)
        rsb = reg.take(T)
        spad = reg.take(4, NB * (CW - 1 + NS))
        after_group = reg.at
        reg.restart(after_stores)
        mhi = reg.take(KT, T, split=True)
        mlo = reg.take(KT, T, split=True)
        after_merged = reg.at
        yhi = reg.take(D_IN // P, T, split=True)
        wab = reg.take(2, P)
        prod = reg.take(2, T)
        reg.restart(after_group)
        gates = reg.take(2, T)
        reg.restart(after_stores)
        hhi = reg.take(FT, T, split=True)
        reg.restart(after_merged)
        part = reg.take(KT, T)
        lsq = reg.take(2, T)
        mean = reg.take(T)
        sdev = reg.take(T)
        rstd = reg.take(T)
        hraw = reg.take(2, T)
        squares = [lsq, hraw]
        xsum = reg.take(T)
        assert reg.at <= after_merged + D_IN // P * T

        acc = [ctx.enter_context(nc.psum_tensor(f"acc{i}", [P, 1024], F32)) for i in range(2)]
        px = ctx.enter_context(nc.psum_tensor("px", [P, 2048], F32))
        px01, px23 = px[:, 0:1024], px[:, 1024:2048]
        X = [px[:, 512 * j:512 * (j + 1)] for j in range(4)]

        def halves(ap):
            return ap.rearrange("p (h n) -> p h n", h=2)

        def two(ps, parts=P):
            return ps[0:parts, :].rearrange("p (h n) -> p h n", h=2)[:, :, 0:HT]

        px_mid = two(px[:, 512:1536])

        def bc(ap, n):
            return ap.unsqueeze(len(ap.shape)).to_broadcast(list(ap.shape) + [n])

        const_ld = sem("const_ld")
        const_set = sem("const_set")
        w_loaded = [sem(f"w_loaded{i}") for i in range(SLOTS)]
        w_hi = [sem(f"w_hi{i}") for i in range(SLOTS)]
        w_split = [sem(f"w_split{i}") for i in range(SLOTS)]
        w_used = [sem(f"w_used{i}") for i in range(SLOTS)]
        acc_done = sem("acc_done")
        acc_free = [sem(f"acc_free{i}") for i in range(2)]
        x_ld, xh_ready, x_ready = sem("x_ld"), sem("xh_ready"), sem("x_ready")
        wdt_ld, wdt_split = sem("wdt_ld"), sem("wdt_split")
        yh_ready, y_split, hh_ready = sem("yh_ready"), sem("y_split"), sem("hh_ready")
        lay_ld = sem("lay_ld")
        dt_exp, wdt_hi_ready, dt_scan, de_ready, tok_t, tok_ready = (
            sem(n) for n in ("dt_exp", "wdt_hi_ready", "dt_scan", "de_ready", "tok_t", "tok_ready"))
        ac_stored = sem("ac_stored")
        rope_raw, rope_sw, rope_px, rope_done = (sem(n) for n in ("rope_raw", "rope_sw", "rope_px", "rope_done"))
        kv_st = sem("kv_st")
        mask_ld, zeroed, qzs_ready = sem("mask_ld"), sem("zeroed"), sem("qzs_ready")
        vt_t, vt_done = sem("vt_t"), sem("vt_done")
        staged, vr_t, vr_done = sem("staged"), sem("vr_t"), sem("vr_done")
        s_max, s_exp, pt_t, pt_done, pv_done, o_norm, ot_t, ot_done = (
            sem(n) for n in ("s_max", "s_exp", "pt_t", "pt_done", "pv_done", "o_norm", "ot_t", "ot_done"))
        c_loaded = [sem(f"c_loaded{i}") for i in range(4)]
        c_used = sem("c_used")
        ss_max, ss_exp, ss_norm, spt_t, spt_done, spv_done, so_copy, so_t, att_done = (
            sem(n) for n in ("ss_max", "ss_exp", "ss_norm", "spt_t", "spt_done", "spv_done", "so_copy", "so_t", "att_done"))
        acb_ld, st_ld = sem("acb_ld"), sem("st_ld")
        gp_ready, post_init, conv_done, th_ready, post_ready, spad_ready, thz_ready, zs_done = (
            sem(n) for n in ("gp_ready", "post_init", "conv_done", "th_ready", "post_ready", "spad_ready",
                             "thz_ready", "zs_done"))
        ea_ready, seg_ready, e_ready, t_done, x0_free, m_ready, pool_step, y_done, h_ready = (
            sem(n) for n in ("ea_ready", "seg_ready", "e_ready", "t_done", "x0_free", "m_ready", "pool_step", "y_done",
                             "h_ready"))
        y_evac, gated, sq_ready, rms_sum, rs_ready, yssm_ready = (
            sem(n) for n in ("y_evac", "gated", "sq_ready", "rms_sum", "rs_ready", "yssm_ready"))
        ns_done, st_dec, ns_add, bm_ready = (sem(n) for n in ("ns_done", "st_dec", "ns_add", "bm_ready"))
        h_st, st_st, cout_st, h_free = (sem(n) for n in ("h_st", "st_st", "cout_st", "h_free"))
        wab_ld, gate_th, mrg_done = sem("wab_ld"), sem("gate_th"), sem("mrg_done")
        relu_done, hid_ready, part_done = sem("relu_done"), sem("hid_ready"), sem("part_done")
        ln_x, ln_sum, ln_mean, ln_c, ln_sq, ln_pair, ln_sqf, ln_sd, ln_n = (
            sem(n) for n in ("ln_x", "ln_sum", "ln_mean", "ln_c", "ln_sq", "ln_pair", "ln_sqf", "ln_sd", "ln_n"))
        y_st = sem("y_st")
        passed = sem("passed")

        def read_of(L, base, pairs, k):
            return L * (TILES // 2) + pairs + (base + k) // 2 + 2

        def all_groups(eng, L, group):
            first = L * GROUPS
            group(0, None, U_GRP, 0, False)
            group(1, first, U_GRP + 6, 0, False)
            with eng.Fori(0, GROUPS // 2 - 1) as i:
                group(2 * i + 2, first + 2 * i + 1, U_GRP + 12, 3 * i, True)
                group(2 * i + 3, first + 2 * i + 2, U_GRP + 18, 3 * i, True)
            group(None, first + GROUPS - 1, None, None, True)

        def hold(eng, s, n):
            eng.wait_ge(s, n)
            eng.sem_inc(passed, 1)

        block = ctx.enter_context(nc.Block())

        @block.sync
        def _(sp):
            sp.dma_start(part, A["x0"]).then_inc(x_ld, 16)
            for name, t in (("ident", ident), ("swap", swap), ("tri", tri), ("tri_s", tri_s), ("bmask", bmask)):
                sp.dma_start(t[:, :], A[name]).then_inc(const_ld, 16)

            def load(L, u, rounds=0):
                slot, use = unit(L, u, rounds)
                sp.wait_ge(w_used[slot], use + 1)
                sp.dma_start(whole[:, slot, :], A["wst"][bass.ds(L * UNITS + u + SLOTS * rounds, 1)].rearrange(
                    "u p n -> (u p) n")).then_inc(w_loaded[slot], 16)

            with sp.Fori(0, DEPTH) as L:
                for u in range(UNITS % (3 * SLOTS)):
                    load(L, u)
                with sp.Fori(0, UNITS // (3 * SLOTS)) as i:
                    for k in range(3 * SLOTS):
                        load(L, UNITS % (3 * SLOTS) + k, 3 * i)
            for u in range(AHEAD):
                slot, use = unit(DEPTH, u)
                sp.wait_ge(w_used[slot], use + 1)
                sp.dma_start(whole[:, slot, :], A["wst"][u]).then_inc(w_loaded[slot], 16)
            sp.wait_ge(x_ready, 16 * DEPTH + 8)
            sp.dma_start(A["y"], part).then_inc(y_st, 16)
            for u in range(AHEAD):
                slot, use = unit(DEPTH, u)
                sp.wait_ge(w_split[slot], use + 1)
            sp.wait_ge(y_st, 16)
            sp.wait_ge(wdt_ld, 32 * DEPTH + 32)

        @block.tensor
        def _(pe):
            pe.wait_ge(const_ld, 16 * 5)
            pe.wait_ge(const_set, 3)

            def claim(L, base, pairs, k):
                pe.wait_ge(acc_free[(base + k) % 2], read_of(L, base, pairs, k) - 1)
                return (base + k) % 2

            def x_parts(k, h):
                cols = slice(h * HT, (h + 1) * HT)
                return xhi[:, k, cols], xlo[:, k, cols]

            def y_parts(k, h):
                cols = slice(h * HT, (h + 1) * HT)
                return yhi[:, k, cols], ylo[:, k, cols]

            def m_parts(k, h):
                cols = slice(h * HT, (h + 1) * HT)
                return mhi[:, k, cols], mlo[:, k, cols]

            def h_parts(k, h):
                cols = slice(h * HT, (h + 1) * HT)
                return hhi[:, k, cols], hlo[:, k, cols]

            def products(out, w_hi_, w_lo_, parts, first, last):
                for h in range(2):
                    hi, lo = parts(h)
                    o = out[:, 512 * h:512 * h + HT]
                    nc.tensor.matmul(o, w_hi_, hi, start=first, stop=False)
                    nc.tensor.matmul(o, w_hi_, lo, start=False, stop=False)
                for h in range(2):
                    mm = nc.tensor.matmul(out[:, 512 * h:512 * h + HT], w_lo_, parts(h)[0], start=False, stop=last)
                return mm

            def gemm(L, base, pairs, k, units, rhs, between=None, ready=None):
                buf = claim(L, base, pairs, k)
                for j, (slot, use) in enumerate(units):
                    pe.wait_ge(w_split[slot], use + 1)
                    for kk in range(KT):
                        cols = slice(kk * P, (kk + 1) * P)
                        if ready is not None:
                            pe.wait_ge(ready[0], ready[1] + 8 * j + kk + 1)
                        mm = products(acc[buf], whi[:, slot, cols], wlo[:, slot, cols],
                                      lambda h: rhs(8 * j + kk, h), j == 0 and kk == 0,
                                      j == len(units) - 1 and kk == KT - 1)
                        if kk == KT - 1:
                            mm.then_inc(w_used[slot], 1)
                        if kk % 2 == 1 and between is not None:
                            between()

            def rope(L, idx, s):
                rho = L * 12 + idx
                pe.wait_ge(rope_raw, rho + 1)
                pe.wait_ge(rope_px, rho + 1)
                for h in range(2):
                    mm = nc.tensor.matmul(px01[:, 512 * h:512 * h + HT], swap[:, :], rraw[:, s, h * HT:(h + 1) * HT],
                                          start=True, stop=True)
                mm.then_inc(rope_sw, 1)

            def layer_norm(n):
                pe.wait_ge(ln_x, n + 1)
                for h in range(2):
                    mm = nc.tensor.matmul(px01[:, 512 * h:512 * h + HT], ones[:, :], xsum[:, h * HT:(h + 1) * HT],
                                          start=True, stop=True)
                mm.then_inc(ln_sum, 1)
                for p in range(KT // 2):
                    pe.wait_ge(ln_pair, 4 * n + p + 1)
                    for h in range(2):
                        mm = nc.tensor.matmul(px23[:, 512 * h:512 * h + HT], ones[:, :],
                                              squares[p % 2][:, 0, h * HT:(h + 1) * HT],
                                              start=p == 0, stop=p == KT // 2 - 1)
                    mm.then_inc(ln_sqf, 1)

            with pe.Fori(0, DEPTH) as L:
                pe.wait_ge(wdt_split, L + 1)
                buf = claim(L, T_DT, 0, 0)
                for k in range(KT):
                    pe.wait_ge(x_ready, 16 * L + k + 1)
                    mm = products(acc[buf][0:HEADS, :], wdt_hi[:, k, :], wdt_lo[:, k, :], lambda h: x_parts(k, h),
                                  k == 0, k == KT - 1)
                mm.then_inc(acc_done, 1)
                for j in range(6):
                    for c in range(3):
                        gemm(L, T_QKV, 0, 3 * j + c, [unit(L, U_QKV + 3 * j + c)], x_parts)
                        if c > 0:
                            rope(L, 2 * j + c - 1, c - 1)
                hold(pe, de_ready, L + 1)
                for c in range(NC + 1):
                    n = CHUNK if c < NC else TS
                    for j in range(3):
                        mm = nc.tensor.transpose(X[2][0:n, (3 * c + j) * HEADS:(3 * c + j + 1) * HEADS],
                                                 dtv[j][:, c * CHUNK:c * CHUNK + n], ident[0:HEADS, 0:HEADS])
                mm.then_inc(tok_t, 1)
                pe.wait_ge(acc_free[0], read_of(L, T_QKV, 6, 5))
                pe.wait_ge(rope_px, 12 * L + 13)
                for j in range(2):
                    for b in range(NC):
                        mm = nc.tensor.transpose(X[j][:, b * P:(b + 1) * P], qkvT[:, 12 + j, b * P:(b + 1) * P],
                                                 ident[:, :])
                    mm.then_inc(vt_t, 1)
                for j in range(4):
                    mm = nc.tensor.transpose(X[3][0:TS, j * P:(j + 1) * P], qkvT[:, 12 + j, SEQ:T], ident[:, :])
                mm.then_inc(vt_t, 1)
                pe.wait_ge(vt_done, 4 * L + 1)
                for j in range(4, 6):
                    mm = nc.tensor.transpose(X[0][0:TS, (j - 4) * P:(j - 3) * P], qkvT[:, 12 + j, SEQ:T], ident[:, :])
                mm.then_inc(vt_t, 1)
                pe.wait_ge(vt_done, 4 * L + 4)
                hold(pe, tok_ready, L + 1)
                def turn_v(r):
                    pe.wait_ge(staged, 4 * L + r + 1)
                    if r > 0:
                        pe.wait_ge(vr_done, 4 * L + r)
                    for j in range(4):
                        mm = nc.tensor.transpose(X[2][:, j * P:(j + 1) * P], vr[:, j, :], ident[:, :])
                    mm.then_inc(vr_t, 1)

                def scores(r, h):
                    buf = claim(L, T_ATT, 2 * r, h)
                    pe.wait_ge(staged, 4 * L + r + 1)
                    nc.tensor.matmul(acc[buf][:, 0:SEQ], qz[:, 0, h, :], qkvT[:, 6 + h // 2, 0:SEQ],
                                     start=True, stop=True)
                    for g in (1, 2):
                        mm = nc.tensor.matmul(acc[buf][:, SEQ + (g - 1) * P:SEQ + g * P], qz[:, g, h, :],
                                              kr[:, 2 * (g - 1) + h // 2, :], start=True, stop=True)
                    mm.then_inc(acc_done, 1)

                def turn_probs(r, h):
                    pe.wait_ge(s_exp, 16 * L + 4 * r + h + 1)
                    pe.wait_ge(pt_done, 16 * L + 4 * r + h + 1)
                    for j in range(6):
                        mm = nc.tensor.transpose(px01[:, j * P:(j + 1) * P], sc[:, h % 2, j * P:(j + 1) * P],
                                                 ident[:, :])
                    mm.then_inc(pt_t, 1)

                def values(r, h):
                    pe.wait_ge(pt_done, 16 * L + 4 * r + h + 2)
                    if h == 0:
                        pe.wait_ge(vr_done, 4 * L + r + 1)
                        pe.wait_ge(ot_done, 4 * L + r + 1)
                    out = X[3][:, h * HD:(h + 1) * HD]
                    for j in range(6):
                        v = (vtok[:, j, h * HD:(h + 1) * HD] if j < 4 else
                             v_res[:, 2 * (j - 4) + h // 2, (h % 2) * HD:(h % 2 + 1) * HD])
                        mm = nc.tensor.matmul(out, pt[:, j * P:(j + 1) * P], v, start=j == 0, stop=j == 5)
                    mm.then_inc(pv_done, 1)

                def turn_out(r):
                    pe.wait_ge(o_norm, 4 * L + r + 2)
                    for j in range(2):
                        mm = nc.tensor.transpose(X[3][:, 256 + j * P:256 + (j + 1) * P], ob[:, j * P:(j + 1) * P],
                                                 ident[:, :])
                    mm.then_inc(ot_t, 1)

                turn_v(0)
                scores(0, 0)
                scores(0, 1)
                for r in range(RES):
                    turn_probs(r, 0)
                    if r > 0:
                        turn_out(r - 1)
                    scores(r, 2)
                    values(r, 0)
                    turn_probs(r, 1)
                    scores(r, 3)
                    values(r, 1)
                    turn_probs(r, 2)
                    values(r, 2)
                    turn_probs(r, 3)
                    if r + 1 < RES:
                        scores(r + 1, 0)
                    values(r, 3)
                    if r + 1 < RES:
                        turn_v(r + 1)
                        scores(r + 1, 1)
                turn_out(RES - 1)
                def sample_scores(bb):
                    buf = T_SMP % 2
                    if bb == 0:
                        claim(L, T_SMP, 0, 0)
                        pe.wait_ge(qzs_ready, L + 1)
                    out = acc[buf][32 * bb:32 * bb + 32, :]
                    for half in range(2):
                        b = 2 * bb + half
                        pe.wait_ge(c_loaded[b % 4], 64 * L + 16 * (b // 4) + 16)
                    terms = [(b, p) for b in (2 * bb, 2 * bb + 1) for p in range(2)]
                    for g, lo, n in ((1, 0, SEQ), (0, SEQ, P), (2, SEQ + P, P)):
                        for b, p in terms:
                            mm = nc.tensor.matmul(out[:, lo:lo + n], qzs[:, g, p, b, :],
                                                  cring[:, b % 4, p * KEYS + lo:p * KEYS + lo + n],
                                                  start=(b, p) == terms[0], stop=(b, p) == terms[-1])
                    mm.then_inc(c_used, 1)
                    for g in range(3):
                        for b, p in terms:
                            mm = nc.tensor.matmul(out[:, KEYS + g * TS:KEYS + (g + 1) * TS], qzs[:, g, p, b, :],
                                                  qkvT[:, 6 + 2 * g + p, SEQ:T],
                                                  start=(b, p) == terms[0], stop=(b, p) == terms[-1])
                    if bb == 3:
                        mm.then_inc(acc_done, 1)

                def sample_turn():
                    pe.wait_ge(ss_norm, L + 1)
                    pe.wait_ge(pt_done, 16 * L + 17)
                    pe.wait_ge(ot_done, 4 * L + 5)
                    for j in range(6):
                        nc.tensor.transpose(px01[:, j * P:(j + 1) * P], sc_s[:, j * P:(j + 1) * P], ident[:, :])
                    for g in range(3):
                        mm = nc.tensor.transpose(X[2][0:TS, g * P:(g + 1) * P],
                                                 sc_s[:, KEYS + g * TS:KEYS + (g + 1) * TS], ident[:, :])
                    mm.then_inc(spt_t, 1)

                def sample_values(bb):
                    if bb == 0:
                        pe.wait_ge(spt_done, L + 1)
                        hold(pe, o_norm, 4 * L + 5)
                    out = X[3][32 * bb:32 * bb + 32, 0:256]
                    for g in range(3):
                        nc.tensor.matmul(out, ptn[:, g, 32 * bb:32 * bb + 32], vtok_s[:, g * 256:(g + 1) * 256],
                                         start=g == 0, stop=False)
                    for half in range(2):
                        b = 2 * bb + half
                        pe.wait_ge(c_loaded[b % 4], 64 * L + 32 + 16 * (b // 4) + 16)
                        for j in range(6):
                            mm = nc.tensor.matmul(out, ptz[:, half, j, 32 * bb:32 * bb + 32],
                                                  cring[:, b % 4, j * 256:(j + 1) * 256],
                                                  start=False, stop=half == 1 and j == 5)
                    mm.then_inc(c_used, 1)

                def sample_out():
                    pe.wait_ge(so_copy, L + 1)
                    for j in range(2):
                        mm = nc.tensor.transpose(X[2][:, j * P:(j + 1) * P], ob[:, j * P:(j + 1) * P], ident[:, :])
                    mm.then_inc(so_t, 1)

                def sample_steps(quarter):
                    if quarter in SAMPLE_K_AT:
                        sample_scores(SAMPLE_K_AT.index(quarter))
                    elif quarter == SAMPLE_TURN_AT:
                        sample_turn()
                    elif quarter in SAMPLE_V_AT:
                        sample_values(SAMPLE_V_AT.index(quarter))
                    elif quarter == SAMPLE_OUT_AT:
                        sample_out()

                def turn(s, c):
                    n = CHUNK if c < NC else TS
                    cols = slice(c * CHUNK, c * CHUNK + n)
                    if c == 0:
                        pe.wait_ge(post_ready, 4 * s + 4)
                    else:
                        pe.wait_ge(x0_free, 5 * s + c)
                    for j, q in enumerate((2, 3, 0)):
                        nc.tensor.transpose(X[0][0:n, j * P:(j + 1) * P], post[:, q, cols], ident[:, :])
                    nc.tensor.matmul(X[0][0:n, 384:384 + n], post[:, 0, cols], post[:, 1, cols],
                                     start=True, stop=True).then_inc(t_done, 1)

                def scan(s, c, late):
                    n = CHUNK if c < NC else TS
                    pe.wait_ge(m_ready, 5 * s + c + 1)
                    pe.wait_ge(pool_step, 5 * s + c + 1)
                    if c == 0 and late:
                        pe.wait_ge(rs_ready, s)
                    if 0 < c < NC:
                        pe.wait_ge(h_ready, 4 * s + c)
                    if c == NC:
                        pe.wait_ge(h_ready, 4 * s + NC)
                        pe.wait_ge(st_ld, 16 * s + 16)
                    for hh in range(HG):
                        rows = slice(HD * (hh % 2), HD * (hh % 2) + HD)
                        hcols = slice(hh * HD, (hh + 1) * HD)
                        out = (X[1 + hh // 2][rows, c * CHUNK:(c + 1) * CHUNK] if c < NC
                               else X[3][rows, 256 + TS * (hh // 2):256 + TS * (hh // 2) + TS])
                        mm = nc.tensor.matmul(out, xdt[0:n, hcols], mdec[0:n, hh, 0:n], start=True,
                                              stop=c in (0, NC))
                        if 0 < c < NC:
                            mm = nc.tensor.matmul(out, hst[:, hcols], cea[:, hh, :], start=False, stop=True)
                        if c == NC:
                            for b in range(NB):
                                mm = nc.tensor.matmul(out[:, b * NS:(b + 1) * NS], st[:, b, hcols],
                                                      cea[:, hh, b * NS:(b + 1) * NS], start=False, stop=True,
                                                      skip_group_check=True)
                    if c < NC:
                        mm = nc.tensor.matmul(X[3][:, 0:256], btok[:, :], xde[:, :], start=True, stop=True)
                    mm.then_inc(y_done, 1)

                def new_states(s, j):
                    if j == 0:
                        pe.wait_ge(x0_free, 5 * s + 5)
                        pe.wait_ge(bm_ready, s + 1)
                    if j == 1:
                        pe.wait_ge(y_evac, 2 * s + 2)
                    if j >= 2:
                        pe.wait_ge(ns_add, 4 * s + j - 1)
                    for b in (2 * j, 2 * j + 1):
                        mm = nc.tensor.matmul(X[3 * (j % 2)][:, (b % 2) * 256:(b % 2 + 1) * 256], bm[:, b, :],
                                              xde[0:TS, :], start=True, stop=True)
                    mm.then_inc(ns_done, 1)

                def rms(s):
                    pe.wait_ge(sq_ready, s + 1)
                    for j in range(2):
                        for h in range(2):
                            mm = nc.tensor.matmul(X[1 + h][:, 0:HT], ones[:, :], sqb[:, j, h * HT:(h + 1) * HT],
                                                  start=j == 0, stop=j == 1)
                    mm.then_inc(rms_sum, 1)

                def scan_steps(s, quarter, late):
                    if quarter == 0:
                        turn(s, 0)
                    elif quarter in SCAN_AT:
                        c = SCAN_AT.index(quarter)
                        if c < NC:
                            turn(s, c + 1)
                        scan(s, c, late)
                    elif quarter in NEW_AT:
                        j = NEW_AT.index(quarter)
                        new_states(s, 2 * j)
                        new_states(s, 2 * j + 1)
                    elif quarter == RMS_AT:
                        rms(s)

                def group(g, s, u, rounds, late):
                    done = [0]

                    def between():
                        done[0] += 1
                        step(done[0])

                    def step(quarter):
                        if s is None:
                            sample_steps(quarter)
                        else:
                            scan_steps(s, quarter, late)

                    step(0)
                    for k in range(6):
                        if g is not None:
                            gemm(L, T_GRP, 3 * g, k, [unit(L, u + k, rounds)], x_parts, between)
                        elif k < 2:
                            gemm(L, T_MRG, 0, k, [unit(L, U_MRG + k)], x_parts, between)
                        else:
                            for _ in range(4):
                                between()

                all_groups(pe, L, group)

                def branches(m):
                    gemm(L, T_MRG, 2 * m, 2, [unit(L, U_MRG + 2, m), unit(L, U_MRG + 3, m)], y_parts,
                         ready=(y_split, 16 * L))
                    buf = claim(L, T_MRG, 2 * m, 3)
                    pe.wait_ge(wab_ld, 16 * (8 * L + m) + 16)
                    for k in range(2):
                        for h in range(2):
                            mm = nc.tensor.matmul(acc[buf][:, 512 * h:512 * h + HT], wab[:, k, :],
                                                  oT[:, k, h * HT:(h + 1) * HT], start=k == 0, stop=k == 1)
                    mm.then_inc(acc_done, 1)

                with pe.Fori(0, KT - 1) as m:
                    branches(m)
                    for k in range(2):
                        gemm(L, T_MRG, 2 * m + 2, k, [unit(L, U_MRG + 4 + k, m)], x_parts)
                branches(KT - 1)
                with pe.Fori(0, 2) as i:
                    for k in range(4):
                        gemm(L, T_WO, 2 * i, k, [unit(L, U_WO + k, i)], m_parts,
                             ready=(mrg_done, 8 * L + 1) if k == 0 else None)
                layer_norm(2 * L)
                for f in range(2):
                    with pe.Fori(0, 4) as i:
                        for k in range(4):
                            gemm(L, T_FFN + 24 * f, 2 * i, k, [unit(L, U_FFN + 32 * f + k, i)], x_parts,
                                 ready=(x_ready, 16 * L + 8) if f == 0 and k == 0 else None)
                    with pe.Fori(0, 4) as i:
                        for k in range(2):
                            u = U_FFN + 32 * f + 16 + 2 * k
                            gemm(L, T_FFN + 24 * f + 16, i, k, [unit(L, u, i), unit(L, u + 1, i)], h_parts,
                                 ready=(hid_ready, 32 * L + 16 * f + 2) if k == 0 else None)
                layer_norm(2 * L + 1)

        @block.scalar
        def _(act):
            act.wait_ge(const_set, 3)

            def unit_done(slot_use):
                slot, use = slot_use
                act.wait_ge(w_used[slot], use + 2)

            def high(L, u, rounds=0):
                slot, use = unit(L, u, rounds)
                act.wait_ge(w_loaded[slot], 16 * use + 16)
                nc.scalar.activation(whi[:, slot, :], whole[:, slot, :], ACT.Copy).then_inc(w_hi[slot], 1)

            def evac(L, base, pairs, k, u, rounds, out, func, **kw):
                high(L, u + AHEAD, rounds)
                unit_done(unit(L, u, rounds))
                b = (base + k) % 2
                nc.scalar.activation(halves(out), two(acc[b]), func, **kw).then_inc(acc_free[b], 1)

            def layer_norm(n, col):
                act.wait_ge(ln_sum, n + 1)
                nc.scalar.activation(halves(mean), two(px01), ACT.Copy, scale=1.0 / D).then_inc(ln_mean, 1)
                for k in range(KT):
                    act.wait_ge(ln_c, 8 * n + k + 1)
                    if k % 2 == 0:
                        act.wait_ge(ln_sqf, 4 * n + k // 2 + 1)
                    nc.scalar.activation(squares[k // 2 % 2][:, k % 2, :], part[:, k, :], ACT.Square)\
                      .then_inc(ln_sq, 1)
                nc.scalar.activation(warm[:, :], eps[:, :], ACT.Sqrt)
                act.wait_ge(ln_sqf, 4 * n + 6)
                nc.scalar.activation(halves(sdev), two(px23), ACT.Sqrt, bias=eps[:, :], scale=1.0 / D)\
                  .then_inc(ln_sd, 1)
                for k in range(KT):
                    act.wait_ge(ln_n, 8 * n + k + 1)
                    gain, bias = lnp[:, col + k:col + k + 1], lnp[:, col + 8 + k:col + 9 + k]
                    nc.scalar.activation(xhi[:, k, :], part[:, k, :], ACT.Identity, bias=bias, scale=gain)
                    act.drain()
                    nc.scalar.activation(part[:, k, :], part[:, k, :], ACT.Identity, bias=bias, scale=gain)\
                      .then_inc(xh_ready, 1)

            def dt_high(L):
                act.wait_ge(wdt_ld, 32 * L + 32)
                nc.scalar.activation(wdt_hi[:, :, :], wdt[:, :, :], ACT.Copy).then_inc(wdt_hi_ready, 1)

            dt_high(0)
            act.wait_ge(x_ld, 16)
            for k in range(KT):
                nc.scalar.activation(xhi[:, k, :], part[:, k, :], ACT.Copy).then_inc(xh_ready, 1)
            for u in range(AHEAD):
                high(0, u)
            with act.Fori(0, DEPTH) as L:
                act.wait_ge(acc_done, COUNTED * L + N_DT + 1)
                nc.scalar.activation(halves(d_e), two(acc[0], HEADS), ACT.Abs, bias=hpar[:, 0:1])
                nc.scalar.activation(halves(d_r), two(acc[0], HEADS), ACT.Relu, bias=hpar[:, 0:1])\
                  .then_inc(acc_free[0], 1)
                act.drain()
                nc.scalar.activation(d_e, d_e, ACT.Exp, scale=-1.0)
                nc.scalar.activation(a_col[:, :], hpar[:, 1:2], ACT.Exp).then_inc(dt_exp, 1)
                for j in range(6):
                    for c in range(3):
                        u = U_QKV + 3 * j + c
                        if c < 2:
                            high(L, u + AHEAD)
                            act.wait_ge(rope_done, 12 * L + 2 * j + c + 1)
                            unit_done(unit(L, u))
                            b = (T_QKV + 3 * j + c) % 2
                            nc.scalar.activation(halves(rraw[:, c, :]), two(acc[b]), ACT.Copy)
                            act.drain().then_inc(acc_free[b], 1)
                            act.sem_inc(rope_raw, 1)
                        else:
                            evac(L, T_QKV, 0, 3 * j + c, u, 0, qkvT[:, 12 + j, :], ACT.Copy)
                    if j == 1:
                        act.wait_ge(dt_scan, L + 1)
                        nc.scalar.activation(de_t, de_t, ACT.Exp).then_inc(de_ready, 1)
                act.drain()
                act.wait_ge(rope_done, 12 * L + 14)
                act.wait_ge(zeroed, L + 1)
                by_class = qkvT[:, :, 0:SEQ].rearrange("p t (n r) -> p t n r", r=RES)
                qz_h = qz.rearrange("p g (q e) n -> p (g q) e n", e=2)
                def stage(r):
                    act.wait_ge(vr_t, 4 * L + r + 1)
                    for e in range(2):
                        rows = slice(HD * e, HD * e + HD)
                        nc.scalar.activation(qz_h[rows, :, e, :], by_class[rows, 0:6, :, r:r + 1].squeeze(), ACT.Copy)
                    nc.scalar.activation(kr, by_class[:, 8:12, :, r:r + 1].squeeze(), ACT.Copy)
                    nc.scalar.activation(vr, by_class[:, 14:18, :, r:r + 1].squeeze(), ACT.Copy)
                    act.drain().then_inc(staged, 1)

                stage(0)
                for r in range(RES):
                    for h in range(4):
                        act.wait_ge(s_max, 16 * L + 4 * r + h + 1)
                        nc.scalar.activation(sc[:, h % 2, :], sc[:, h % 2, :], ACT.Exp, bias=rowmax[:, h:h + 1],
                                             accum_out=rowsum[:, r % 2, h:h + 1])
                        act.drain().then_inc(s_exp, 1)
                    if r + 1 < RES:
                        act.wait_ge(acc_done, COUNTED * L + N_ATT + 4 * r + 4)
                        stage(r + 1)

                def gate(m, k):
                    high(L, U_MRG + k + AHEAD, m)
                    unit_done(unit(L, U_MRG + k, m))
                    b = (T_MRG + k) % 2
                    nc.scalar.activation(halves(gates[:, k, :]), two(acc[b]), ACT.Tanh, scale=0.5)
                    act.drain().then_inc(acc_free[b], 1)
                    act.sem_inc(gate_th, 1)

                def group(g, s, u, rounds, late):
                    c = None if g is None else L * GROUPS + g

                    def conv_init(q):
                        nc.scalar.activation(post[:, q, :], raw[:, q, :], ACT.Identity,
                                             bias=gconv[:, 16 + q:17 + q], scale=gconv[:, 4 * q + 3:4 * q + 4])\
                          .then_inc(post_init, 1)

                    def conv_act(q):
                        act.wait_ge(conv_done, 4 * c + q + 1)
                        if q >= 2:
                            act.wait_ge(post_ready, 4 * c + q - 1)
                        nc.scalar.activation(th[:, q % 2, :], post[:, q, :], ACT.Tanh).then_inc(th_ready, 1)

                    def decay(k):
                        n = CHUNK if k < NC else TS
                        act.wait_ge(seg_ready, 5 * s + k + 1)
                        v = seg[0:n, k % 2, :, 0:n]
                        nc.scalar.activation(v, v, ACT.Exp).then_inc(e_ready, 1)

                    def tile(k):
                        if s is not None:
                            if k < 4:
                                act.wait_ge(conv_done, 4 * c - 4 + k + 1)
                            elif k == 4:
                                act.wait_ge(zs_done, s + 1)
                        evac(L, T_GRP, 3 * g, k, u + k, rounds, raw[:, k, :], ACT.Copy, scale=1.0 if k < 4 else 0.5)

                    if s is not None:
                        act.drain()
                        decay(0)
                        act.wait_ge(acb_ld, 16 * s + 16)
                        nc.scalar.activation(ea, acb, ACT.Exp).then_inc(ea_ready, 1)
                        decay(1)
                        nc.scalar.activation(thz, raw[:, 4:6, :], ACT.Tanh).then_inc(thz_ready, 1)
                    if g is not None:
                        tile(0)
                    if s is None:
                        act.wait_ge(ss_max, L + 1)
                        nc.scalar.activation(sc_s, sc_s, ACT.Exp, bias=rowmax[:, 0:1], accum_out=rowsum[:, 0, 0:1])
                        act.drain().then_inc(ss_exp, 1)
                    if s is not None:
                        decay(2)
                    if g is not None:
                        tile(1)
                    if s is not None:
                        decay(3)
                        decay(4)
                    if g is not None:
                        tile(2)
                        if s is None:
                            tile(3)
                        act.drain()
                        act.wait_ge(gp_ready, c + 1)
                    if s is None:
                        act.wait_ge(kv_st, 16 * L + 16)
                        act.wait_ge(att_done, L + 1)
                    if s is not None:
                        act.wait_ge(y_evac, 2 * s + 2)
                    if g is not None:
                        conv_init(0)
                        conv_init(1)
                        conv_init(2)
                    if s is not None:
                        act.wait_ge(gated, s + 1)
                        nc.scalar.activation(sqb, yg, ACT.Square).then_inc(sq_ready, 1)
                    if g is None:
                        gate(0, 0)
                        gate(0, 1)
                    if g is not None:
                        conv_act(0)
                        conv_act(1)
                        conv_act(2)
                        if s is not None:
                            tile(3)
                        act.drain()
                        conv_init(3)
                    if s is not None:
                        act.wait_ge(rms_sum, s + 1)
                        nc.scalar.activation(halves(rsb), px_mid, ACT.Sqrt, bias=eps[:, :], scale=1.0 / 256)\
                          .then_inc(rs_ready, 1)
                    if g is not None:
                        conv_act(3)
                        tile(4)
                        tile(5)

                all_groups(act, L, group)
                act.wait_ge(yssm_ready, 16 * L + 16)
                for k in range(D_IN // P):
                    nc.scalar.activation(yhi[:, k, :], yssm[:, k, :], ACT.Copy).then_inc(yh_ready, 1)
                with act.Fori(0, KT - 1) as m:
                    high(L, U_MRG + 2 + AHEAD, m)
                    high(L, U_MRG + 3 + AHEAD, m)
                    act.wait_ge(mrg_done, 8 * L + m + 2)
                    gate(m + 1, 0)
                    gate(m + 1, 1)
                high(L, U_MRG + 2 + AHEAD, KT - 1)
                high(L, U_MRG + 3 + AHEAD, KT - 1)
                with act.Fori(0, 2) as i:
                    for k in range(4):
                        high(L, U_WO + k + AHEAD, i)
                layer_norm(2 * L, 0)
                for f in range(2):
                    with act.Fori(0, 4) as i:
                        for k in range(4):
                            u = U_FFN + 32 * f + k
                            idx = 32 * L + 16 * f + 4 * i + k
                            act.wait_ge(hid_ready, idx - 1 + 2)
                            evac(L, T_FFN + 24 * f, 2 * i, k, u, i, hraw[:, k % 2, :], ACT.Relu)
                            act.drain()
                            nc.scalar.activation(hhi[:, bass.ds(4 * i + k, 1), :].rearrange("p a n -> p (a n)"),
                                                 hraw[:, k % 2, :], ACT.Square).then_inc(hh_ready, 1)
                    with act.Fori(0, 4 - f) as i:
                        for k in range(4):
                            high(L, U_FFN + 32 * f + 16 + k + AHEAD, i)
                for u in range(UNITS - SLOTS + AHEAD, UNITS):
                    high(L, u)
                for u in range(AHEAD):
                    high(L + 1, u)
                dt_high(L + 1)
                layer_norm(2 * L + 1, 16)

        @block.vector
        def _(dve):
            nc.vector.memset(ones[:, :], 1.0)
            nc.vector.memset(eps[:, :], EPS)
            nc.vector.memset(tokm[:, :, :, :], 0.0)
            dve.drain().then_inc(const_set, 3)
            dve.wait_ge(const_ld, 16 * 5)

            def x_low(n):
                for k in range(KT):
                    dve.wait_ge(xh_ready, 8 * n + k + 1)
                    nc.vector.tensor_tensor(xlo[:, k, :], part[:, k, :], xhi[:, k, :].bitcast(F32), ALU.subtract)\
                      .then_inc(x_ready, 1)

            def layer_norm(n):
                dve.wait_ge(ln_mean, n + 1)
                for k in range(KT):
                    nc.vector.tensor_tensor(part[:, k, :], part[:, k, :], mean, ALU.subtract).then_inc(ln_c, 1)
                    for p in {3: (0,), 5: (1,), 7: (2, 3)}.get(k, ()):
                        dve.wait_ge(ln_sq, 8 * n + 2 * p + 2)
                        v = squares[p % 2]
                        nc.vector.tensor_tensor(v[:, 0, :], v[:, 0, :], v[:, 1, :], ALU.add).then_inc(ln_pair, 1)
                dve.wait_ge(ln_sd, n + 1)
                nc.vector.reciprocal(rstd, sdev)
                dve.drain()
                for k in range(KT):
                    nc.vector.tensor_tensor(part[:, k, :], part[:, k, :], rstd, ALU.mult).then_inc(ln_n, 1)
                x_low(n + 1)

            def residual(m, b):
                hi, lo, p = (v[:, bass.ds(m, 1), :].rearrange("p a n -> p (a n)") for v in (xhi, xlo, part))
                nc.vector.scalar_tensor_tensor(halves(p), halves(hi.bitcast(F32)), ALPHA, two(acc[b]), ALU.mult, ALU.add)
                dve.drain().then_inc(acc_free[b], 1)
                nc.vector.scalar_tensor_tensor(p, lo.bitcast(F32), ALPHA, p, ALU.mult, ALU.add)
                dve.drain()

            def add_up(m):
                nc.vector.tensor_tensor(xsum, xsum, part[:, bass.ds(m, 1), :].rearrange("p a n -> p (a n)"), ALU.add)
                dve.drain()

            def unit_done(slot_use):
                slot, use = slot_use
                dve.wait_ge(w_used[slot], use + 2)

            def dt_low(L):
                dve.wait_ge(wdt_hi_ready, L + 1)
                nc.vector.tensor_tensor(wdt_lo[:, :, :], wdt[:, :, :], wdt_hi[:, :, :].bitcast(F32), ALU.subtract)\
                  .then_inc(wdt_split, 1)

            dt_low(0)
            x_low(0)
            with dve.Fori(0, DEPTH) as L:
                dve.wait_ge(dt_exp, L + 1)
                nc.vector.tensor_scalar(d_z, d_e, 2.0, None, ALU.add)
                dve.drain()
                nc.vector.reciprocal(d_z, d_z)
                dve.drain()
                nc.vector.tensor_tensor(d_z, d_z, d_e, ALU.mult)
                dve.drain()
                nc.vector.tensor_tensor(d_z2, d_z, d_z, ALU.mult)
                dve.drain()
                nc.vector.tensor_scalar(d_e, d_z2, 2.0 / 17, None, ALU.mult)
                for j in range(7, 0, -1):
                    dve.drain()
                    nc.vector.scalar_tensor_tensor(d_e, d_e, 2.0 / (2 * j + 1), d_z2, ALU.add, ALU.mult)
                dve.drain()
                nc.vector.scalar_tensor_tensor(d_e, d_e, 2.0, d_z, ALU.add, ALU.mult)
                dve.drain()
                nc.vector.tensor_tensor(dt_t, d_e, d_r, ALU.add)
                dve.drain()
                nc.vector.tensor_scalar(d_z, dt_t, a_col[:, 0:1], -1.0, ALU.mult, ALU.mult)
                dve.drain()
                dve.wait_ge(lay_ld, 96 * L + 96)
                nc.vector.tensor_tensor_scan(ac_t, restarts, d_z, 0.0, ALU.mult, ALU.add)
                dve.drain()
                for lo, a, b in ((0, NC, CHUNK), (SEQ, NB, NS)):
                    v = ac_t[:, lo:lo + a * b].rearrange("p (a b) -> p a b", a=a)
                    w = de_t[:, lo:lo + a * b].rearrange("p (a b) -> p a b", a=a)
                    end = v[:, :, b - 1:b].to_broadcast([HEADS, a, b])
                    nc.vector.tensor_tensor(w, end, v, ALU.subtract)
                dve.drain().then_inc(dt_scan, 1)
                for j in range(6):
                    for c in range(2):
                        rho = 12 * L + 2 * j + c
                        dve.wait_ge(rope_sw, rho + 1)
                        out = qkvT[:, 6 * c + j, :]
                        nc.vector.tensor_tensor(halves(rtmp), two(px01), halves(sinT), ALU.mult)\
                          .then_inc(rope_px, 1)
                        nc.vector.tensor_tensor(out, rraw[:, c, :], cosT, ALU.mult)
                        dve.drain()
                        nc.vector.tensor_tensor(out, out, rtmp, ALU.add)
                        dve.drain().then_inc(rope_done, 1)
                dve.wait_ge(tok_t, L + 1)
                per = 3 * HEADS
                nc.vector.tensor_copy(tokm[:, 0:NC, :, :].rearrange("p a b c -> p (a b c)"), X[2][:, 0:NC * per])
                nc.vector.tensor_copy(tokm[0:TS, NC, :, :].rearrange("p b c -> p (b c)"),
                                      X[2][0:TS, NC * per:(NC + 1) * per])
                dve.drain().then_inc(tok_ready, 1)
                for j in range(2):
                    dve.wait_ge(vt_t, 4 * L + j + 1)
                    nc.vector.tensor_copy(vtok[:, :, j * P:(j + 1) * P], X[j].rearrange("p (b n) -> p b n", b=NC))\
                      .then_inc(vt_done, 1)
                dve.wait_ge(vt_t, 4 * L + 3)
                nc.vector.tensor_copy(vtok_s[:, 0:512], X[3][0:TS, :]).then_inc(vt_done, 1)
                dve.wait_ge(vt_t, 4 * L + 4)
                nc.vector.tensor_copy(vtok_s[:, 512:768], X[0][0:TS, 0:256]).then_inc(vt_done, 1)
                dve.wait_ge(mask_ld, 32 * L + 32)

                def v_class(r):
                    dve.wait_ge(vr_t, 4 * L + r + 2)
                    nc.vector.tensor_copy(v_res.rearrange("p a n -> p (a n)"), X[2]).then_inc(vr_done, 1)

                def softmax(r, h):
                    idx = 16 * L + 4 * r + h
                    b = (T_ATT + h) % 2
                    dve.wait_ge(acc_done, COUNTED * L + N_ATT + 4 * r + h + 1)
                    dve.wait_ge(pt_t, idx - 1 + 2)
                    nc.vector.scalar_tensor_tensor(sc[:, h % 2, :], acc[b][:, 0:KEYS], HD ** -0.5, mask[:, r, :],
                                                   ALU.mult, ALU.add).then_inc(acc_free[b], 1)
                    dve.drain()
                    nc.vector.tensor_reduce(rowmax[:, h:h + 1], sc[:, h % 2, :], AX_X, ALU.max, negate=True)\
                      .then_inc(s_max, 1)

                def probs(r, h):
                    idx = 16 * L + 4 * r + h
                    dve.wait_ge(pt_t, idx + 3)
                    dve.wait_ge(pv_done, idx + 1)
                    nc.vector.tensor_copy(pt, px01[:, 0:KEYS]).then_inc(pt_done, 1)

                def normalise(r):
                    nc.vector.reciprocal(rowinv, rowsum[:, r % 2, :])
                    dve.drain()
                    dve.wait_ge(pv_done, 16 * L + 4 * r + 5)
                    nc.vector.tensor_tensor(ob.rearrange("p (h n) -> p h n", h=HG),
                                            X[3][:, 0:256].rearrange("p (h n) -> p h n", h=HG), bc(rowinv, HD),
                                            ALU.mult).then_inc(o_norm, 1)

                def output(r):
                    dve.wait_ge(ot_t, 4 * L + r + 1)
                    nc.vector.tensor_copy(
                        oT[:, :, 0:SEQ].rearrange("p t (n r) -> p t n r", r=RES)[:, :, :, r:r + 1].squeeze(),
                        X[3][:, 256:512].rearrange("p (t n) -> p t n", t=2)).then_inc(ot_done, 1)

                v_class(0)
                softmax(0, 0)
                softmax(0, 1)
                for r in range(RES):
                    probs(r, 0)
                    if r > 0:
                        output(r - 1)
                    softmax(r, 2)
                    probs(r, 1)
                    softmax(r, 3)
                    probs(r, 2)
                    probs(r, 3)
                    if r + 1 < RES:
                        softmax(r + 1, 0)
                    normalise(r)
                    if r + 1 < RES:
                        v_class(r + 1)
                        softmax(r + 1, 1)
                output(RES - 1)
                b = T_SMP % 2
                dve.wait_ge(acc_done, COUNTED * L + N_SMP + 1)
                nc.vector.scalar_tensor_tensor(sc_s, acc[b][:, 0:SKEYS], HD ** -0.5, mask_s, ALU.mult, ALU.add)\
                  .then_inc(acc_free[b], 1)
                dve.drain()
                nc.vector.tensor_reduce(rowmax[:, 0:1], sc_s, AX_X, ALU.max, negate=True).then_inc(ss_max, 1)
                dve.wait_ge(ss_exp, L + 1)
                nc.vector.reciprocal(rowinv[:, 0:1], rowsum[:, 0, 0:1])
                dve.drain()
                nc.vector.tensor_scalar(sc_s, sc_s, rowinv[:, 0:1], None, ALU.mult).then_inc(ss_norm, 1)
                dve.wait_ge(spt_t, L + 1)
                for half in range(2):
                    out = ptz[:, half].rearrange("p k (q e n) -> p k q e n", q=4, e=2)[:, :, :, half, :]
                    src = px01[:, 0:KEYS].rearrange("p (k q e n) -> p k q e n", k=6, q=4, e=2)[:, :, :, half, :]
                    nc.vector.tensor_copy(out, src)
                nc.vector.tensor_copy(ptn, X[2][0:TS, 0:3 * P].rearrange("p (g n) -> p g n", g=3))
                dve.drain().then_inc(spt_done, 1)
                dve.wait_ge(c_used, 8 * L + 8)
                nc.vector.tensor_copy(ob, X[3][:, 0:256]).then_inc(so_copy, 1)
                dve.wait_ge(so_t, L + 1)
                for h in range(HG):
                    rows = slice(HD * (h % 2), HD * (h % 2) + HD)
                    src = X[2][rows, (h // 2) * P:(h // 2 + 1) * P].rearrange("p (b h t) -> p b h t", b=NB, h=HG)
                    nc.vector.tensor_copy(oT[rows, h // 2, SEQ:T].rearrange("p (b t) -> p b t", b=NB), src[:, :, h, :])
                dve.drain().then_inc(att_done, 1)

                def group(g, s, u, rounds, late):
                    c = None if g is None else L * GROUPS + g
                    gs = GROUPS - 1 if g is None else g - 1

                    def conv(q):
                        dve.wait_ge(post_init, 4 * c + q + 1)
                        dve.wait_ge(spad_ready, 4 * c + q + 1)
                        u = post[:, q, :]
                        us = u[:, SEQ:T].rearrange("p (b t) -> p b t", b=NB)
                        pad = spad[:, q].rearrange("p (b t) -> p b t", b=NB)
                        for tap in (2, 1, 0):
                            lag = CW - 1 - tap
                            w = gconv[:, 4 * q + tap:4 * q + tap + 1]
                            nc.vector.scalar_tensor_tensor(u[:, lag:SEQ], raw[:, q, 0:SEQ - lag], w, u[:, lag:SEQ],
                                                           ALU.mult, ALU.add)
                            nc.vector.scalar_tensor_tensor(us, pad[:, :, tap:tap + NS], w, us, ALU.mult, ALU.add)
                            if tap:
                                dve.drain()
                        dve.drain().then_inc(conv_done, 1)

                    def silu(q):
                        dve.wait_ge(th_ready, 4 * c + q + 1)
                        nc.vector.scalar_tensor_tensor(post[:, q, :], th[:, q % 2, :], 1.0, post[:, q, :],
                                                       ALU.add, ALU.mult).then_inc(post_ready, 1)

                    def exponents(k):
                        n = CHUNK if k < NC else TS
                        for hh in range(HG):
                            nc.vector.tensor_scalar(seg[0:n, k % 2, hh, 0:n], acb[0:n, hh, k * CHUNK:k * CHUNK + n],
                                                    gt[0:n, k, 1, hh:hh + 1], 0.0, ALU.subtract, ALU.min)
                        dve.drain().then_inc(seg_ready, 1)

                    def chunk(k):
                        n = CHUNK if k < NC else TS
                        dve.wait_ge(t_done, 5 * s + k + 1)
                        nc.vector.tensor_tensor(xdt[0:n, :].rearrange("p (h d) -> p h d", h=HG),
                                                X[0][0:n, 0:256].rearrange("p (h d) -> p h d", h=HG),
                                                bc(gt[0:n, k, 0, :], HD), ALU.mult)
                        nc.vector.tensor_copy(btok[0:n, :], X[0][0:n, 256:384])
                        nc.vector.tensor_tensor(cbm[0:n, 0:n], X[0][0:n, 384:384 + n],
                                                (tri if k < NC else tri_s)[0:n, 0:n], ALU.mult)
                        dve.drain().then_inc(x0_free, 1)
                        dve.wait_ge(e_ready, 5 * s + k + 1)
                        nc.vector.tensor_tensor(mdec[0:n, :, 0:n], seg[0:n, k % 2, :, 0:n],
                                                cbm[0:n, 0:n].unsqueeze(1).to_broadcast([n, HG, n]), ALU.mult)\
                          .then_inc(m_ready, 1)
                        if k + 2 <= NC:
                            dve.drain()
                            exponents(k + 2)
                        between_scans(k)
                        if k == NC:
                            return
                        hv = hst.rearrange("p (h d) -> p h d", h=HG)
                        dve.wait_ge(y_done, 5 * s + k + 1)
                        if k > 0:
                            last = (k + 1) * CHUNK - 1
                            nc.vector.tensor_tensor(hv, hv, ea[:, :, last:last + 1].to_broadcast([P, HG, HD]), ALU.mult)
                            dve.drain()
                            nc.vector.tensor_tensor(hst, hst, X[3][:, 0:256], ALU.add).then_inc(h_ready, 1)
                        else:
                            dve.wait_ge(h_free, s + 1)
                            nc.vector.tensor_copy(hst, X[3][:, 0:256]).then_inc(h_ready, 1)

                    def add_states(j):
                        dve.wait_ge(ns_done, 4 * s + j + 1)
                        v = st[:, 2 * j:2 * j + 2, :].rearrange("p b n -> p (b n)")
                        nc.vector.tensor_tensor(v, v, X[3 * (j % 2)], ALU.add).then_inc(ns_add, 1)

                    def norm_inverse(s, h):
                        dve.wait_ge(rs_ready, s + 1)
                        nc.vector.reciprocal(rsb[:, h * HT:(h + 1) * HT], rsb[:, h * HT:(h + 1) * HT])

                    def norm_scale(gs, j):
                        dve.drain()
                        nc.vector.scalar_tensor_tensor(
                            yssm[:, bass.ds(2 * gs + j, 1), :].rearrange("p a n -> p (a n)"), yg[:, j, :],
                            par[:, bass.ds(gs, 1), 22 + j:23 + j].rearrange("p a n -> p (a n)"), rsb,
                            ALU.mult, ALU.mult).then_inc(yssm_ready, 1)

                    def between_scans(k):
                        if late and k < 2:
                            norm_inverse(s - 1, k)
                        elif late and k < 4:
                            norm_scale(gs - 1, k - 2)
                        if k == NC:
                            dve.wait_ge(thz_ready, s + 1)
                            nc.vector.scalar_tensor_tensor(zs, thz, 1.0, raw[:, 4:6, :], ALU.add, ALU.mult)\
                              .then_inc(zs_done, 1)

                    dve.drain()
                    if s is not None:
                        nc.vector.tensor_copy(gt[:, :, :, :].rearrange("p a b c -> p (a b) c"),
                                              tokm[:, :, :, bass.ds(gs * HG, HG)].rearrange("p a b c -> p (a b) c"))
                        nc.vector.tensor_copy(gp[:, :], par[:, bass.ds(gs, 1), 20:22].rearrange("p a n -> p (a n)"))
                        dve.drain()
                        dve.wait_ge(acb_ld, 16 * s + 16)
                        exponents(0)
                        exponents(1)
                        dve.wait_ge(ea_ready, s + 1)
                        for k in range(NC + 1):
                            chunk(k)
                            if k == NC - 1:
                                for j in range(2):
                                    ins = nc.vector.scalar_tensor_tensor(yg[:, j, 0:SEQ], post[:, 2 + j, 0:SEQ],
                                                                         gp[:, j:j + 1], X[1 + j], ALU.mult, ALU.add)
                                ins.then_inc(y_evac, 1)
                        dve.wait_ge(y_done, 5 * s + 5)
                        for j in range(2):
                            ins = nc.vector.scalar_tensor_tensor(yg[:, j, SEQ:T], post[:, 2 + j, SEQ:T], gp[:, j:j + 1],
                                                                 X[3][:, 256 + TS * j:256 + TS * (j + 1)],
                                                                 ALU.mult, ALU.add)
                        ins.then_inc(y_evac, 1)
                        dve.drain()
                        nc.vector.tensor_tensor(yg, yg, zs, ALU.mult).then_inc(gated, 1)
                    if g is not None:
                        nc.vector.tensor_scalar(gconv[:, :], par[:, bass.ds(g, 1), 0:20].rearrange("p a n -> p (a n)"),
                                                0.5, None, ALU.mult)
                        dve.drain().then_inc(gp_ready, 1)
                        conv(0)
                    if s is not None:
                        dve.wait_ge(st_dec, s + 1)
                        add_states(0)
                        add_states(1)
                    if g is not None:
                        conv(1)
                        silu(0)
                        conv(2)
                        silu(1)
                    if s is not None:
                        add_states(2)
                        add_states(3)
                    if g is not None:
                        conv(3)
                        silu(2)
                        silu(3)
                    else:
                        for h in range(2):
                            norm_inverse(s, h)
                        for j in range(2):
                            norm_scale(gs, j)

                all_groups(dve, L, group)

                for k in range(D_IN // P):
                    dve.wait_ge(yh_ready, 16 * L + k + 1)
                    nc.vector.tensor_tensor(ylo[:, k, :], yssm[:, k, :], yhi[:, k, :].bitcast(F32), ALU.subtract)\
                      .then_inc(y_split, 1)
                with dve.Fori(0, KT) as m:
                    dve.drain()
                    for k in range(2):
                        dve.wait_ge(gate_th, 16 * L + 2 * m + k + 1)
                        nc.vector.tensor_scalar(gates[:, k, :], gates[:, k, :], 0.5, 0.5, ALU.mult, ALU.add)
                    dve.drain()
                    unit_done(unit(L, U_MRG + 3, m))
                    b = (T_MRG + 2) % 2
                    nc.vector.tensor_tensor(halves(prod[:, 0, :]), two(acc[b]), halves(gates[:, 0, :]), ALU.mult)\
                      .then_inc(acc_free[b], 1)
                    dve.wait_ge(acc_done, COUNTED * L + N_MRG + m + 1)
                    nc.vector.tensor_tensor(halves(prod[:, 1, :]), two(acc[1 - b]), halves(gates[:, 1, :]), ALU.mult)\
                      .then_inc(acc_free[1 - b], 1)
                    dve.drain()
                    nc.vector.tensor_tensor(prod[:, 0, :], prod[:, 0, :], prod[:, 1, :], ALU.add)
                    dve.drain()
                    hi, lo = (v[:, bass.ds(m, 1), :].rearrange("p a n -> p (a n)") for v in (mhi, mlo))
                    nc.vector.tensor_copy(hi, prod[:, 0, :])
                    dve.drain()
                    nc.vector.tensor_tensor(lo, prod[:, 0, :], hi.bitcast(F32), ALU.subtract).then_inc(mrg_done, 1)
                nc.vector.memset(xsum, 0.0)
                dve.drain()
                with dve.Fori(0, 2) as i:
                    for k in range(4):
                        unit_done(unit(L, U_WO + k, i))
                        residual(4 * i + k, (T_WO + k) % 2)
                        add_up(4 * i + k)
                dve.sem_inc(ln_x, 1)
                layer_norm(2 * L)
                nc.vector.memset(xsum, 0.0)
                dve.drain()
                for f in range(2):
                    with dve.Fori(0, 4) as i:
                        for k in range(4):
                            dve.wait_ge(hh_ready, 32 * L + 16 * f + 4 * i + k + 1)
                            v = hraw[:, k % 2, :]
                            hi, lo = (h[:, bass.ds(4 * i + k, 1), :].rearrange("p a n -> p (a n)") for h in (hhi, hlo))
                            nc.vector.tensor_tensor(v, v, v, ALU.mult)
                            dve.drain()
                            nc.vector.tensor_tensor(lo, v, hi.bitcast(F32), ALU.subtract).then_inc(hid_ready, 1)
                    with dve.Fori(0, 4) as i:
                        for k in range(2):
                            unit_done(unit(L, U_FFN + 32 * f + 16 + 2 * k + 1, i))
                            b = (T_FFN + k) % 2
                            if f == 0:
                                residual(2 * i + k, b)
                            else:
                                p = halves(part[:, bass.ds(2 * i + k, 1), :].rearrange("p a n -> p (a n)"))
                                nc.vector.tensor_tensor(p, p, two(acc[b]), ALU.add)
                                dve.drain().then_inc(acc_free[b], 1)
                                add_up(2 * i + k)
                dve.sem_inc(ln_x, 1)
                dt_low(L + 1)
                layer_norm(2 * L + 1)

        @block.gpsimd
        def _(pool):
            for s_, n in ([(w, 1) for w in w_used] + [(a, 1) for a in acc_free] +
                          [(rope_px, 1), (rope_done, 2), (vr_t, 1), (pt_t, 2), (pt_done, 1), (pv_done, 1), (o_norm, 1),
                           (ot_done, 1), (mrg_done, 1), (hid_ready, 2), (ln_sqf, 2), (h_free, 1)]):
                pool.sem_inc(s_, n)

            def row(ap, i, pat):
                return ap[bass.ds(i, 1)].rearrange(pat)

            def low(L, u, rounds=0):
                slot, use = unit(L, u, rounds)
                pool.wait_ge(w_hi[slot], use + 1)
                pool.tensor_tensor(wlo[:, slot, :], whole[:, slot, :], whi[:, slot, :].bitcast(F32), ALU.subtract)\
                    .then_inc(w_split[slot], 1)

            def load_dt(L):
                pool.dma_start(wdt[:, :, :], row(A["wdt"], L, "o p a b -> (o p) a b")).then_inc(wdt_ld, 16)
                pool.dma_start(hpar[:, :], row(A["hpar"], L, "o p a -> (o p) a")).then_inc(wdt_ld, 16)

            load_dt(0)
            for u in range(AHEAD):
                low(0, u)
            with pool.Fori(0, DEPTH) as L:
                hold(pool, x_ready, 16 * L + 8)
                for t, name in ((restarts, "restart"), (cosT, "cos"), (sinT, "sin")):
                    pool.dma_start(t, A[name]).then_inc(lay_ld, 16)
                pool.dma_start(lnp[:, :], row(A["lnp"], L, "o p a -> (o p) a")).then_inc(lay_ld, 16)
                for t, name in ((par, "par"), (cst, "cst")):
                    pool.dma_start(t[:, :, :], row(A[name], L, "o p a b -> (o p) a b")).then_inc(lay_ld, 16)
                pool.dma_start(mask.bitcast(U16), A["mask"]).then_inc(mask_ld, 16)
                pool.dma_start(mask_s.bitcast(U16), A["mask_s"]).then_inc(mask_ld, 16)
                pool.memset(qz, 0.0)
                pool.memset(qzs, 0.0)
                pool.drain().then_inc(zeroed, 1)
                for k in range(U_GRP):
                    low(L, U_QKV + k + AHEAD)
                hold(pool, dt_scan, L + 1)
                pool.dma_start(A["ac"], ac_t).then_inc(ac_stored, 16)
                hold(pool, tok_ready, L + 1)
                hold(pool, ac_stored, 16 * L + 16)
                pool.memset(ptz, 0.0)
                for b in range(4):
                    pool.dma_start(cring[:, b, :], row(A["kc"], L * NB + b, "o p n -> (o p) n")).then_inc(c_loaded[b], 16)
                hold(pool, rope_done, 12 * L + 14)
                pool.drain()
                for e in range(2):
                    rows = slice(HD * e, HD * e + HD)
                    for p in range(2):
                        for half in range(2):
                            at = half * 16 + (2 * p + e) * NS
                            out = qzs[rows, :, p].rearrange("d g (q w) n -> d g q w n", w=2)[:, :, :, half, at:at + NS]
                            src = qkvT[rows, 0:6, SEQ:T].rearrange("d (g p) (q w t) -> d g p q w t", p=2, q=4, w=2)[
                                :, :, p, :, half, :]
                            pool.tensor_copy(out, src)
                pool.drain().then_inc(qzs_ready, 1)
                hold(pool, acc_free[0], read_of(L, T_QKV, 6, 5))
                pool.dma_start(row(A["kv"], L, "o p t n -> (o p) t n"), qkvT[:, 6:18, :]).then_inc(kv_st, 16)
                for b in range(4, 8):
                    hold(pool, c_used, 8 * L + b // 2 - 1)
                    pool.dma_start(cring[:, b % 4, :], row(A["kc"], L * NB + b, "o p n -> (o p) n"))\
                        .then_inc(c_loaded[b % 4], 16)
                for b in range(8):
                    if b == 4:
                        for k in range(3):
                            low(L, U_GRP + k + AHEAD)
                    hold(pool, c_used, 8 * L + b // 2 + 3)
                    pool.dma_start(cring[:, b % 4, :], row(A["vc"], L * NB + b, "o p n -> (o p) n"))\
                        .then_inc(c_loaded[b % 4], 16)
                hold(pool, kv_st, 16 * L + 16)
                hold(pool, att_done, L + 1)

                def load_decay(gi, s):
                    pool.dma_start(acb, A["ac"][bass.ds(gi * HG, HG), :].partition_broadcast(P)).then_inc(acb_ld, 16)

                def load_state(gi, s):
                    pool.dma_start(st, row(A["st"], s, "o p b n -> (o p) b n")).then_inc(st_ld, 16)

                def pad_of(g, q):
                    c = L * GROUPS + g
                    hold(pool, acc_free[q % 2], read_of(L, T_GRP, 3 * g, q))
                    pad = spad[:, q].rearrange("p (b t) -> p b t", b=NB)
                    pool.tensor_copy(pad[:, :, CW - 1:], raw[:, q, SEQ:T].rearrange("p (b t) -> p b t", b=NB))
                    pool.tensor_copy(pad[:, :, 0:CW - 1], cst[:, bass.ds(4 * g + q, 1), :].rearrange(
                        "p a (b t) -> p (a b) t", b=NB))
                    pool.tensor_copy(cout[:, q, :], raw[:, q, T - 35:T])
                    pool.drain().then_inc(spad_ready, 1)
                    if q == 3:
                        pool.dma_start(row(A["cout"], c, "o p q n -> (o p) q n"), cout).then_inc(cout_st, 16)

                def side(s, k):
                    n = CHUNK if k < NC else TS
                    hold(pool, x0_free, 5 * s + k + 1)
                    cols = slice(k * CHUNK, k * CHUNK + n)

                    def weigh_x():
                        pool.tensor_tensor(xde[0:n, :].rearrange("p (h d) -> p h d", h=HG),
                                           xdt[0:n, :].rearrange("p (h d) -> p h d", h=HG), bc(gt[0:n, k, 2, :], HD),
                                           ALU.mult)

                    if k < NC:
                        weigh_x()
                    if k > 0:
                        pool.tensor_tensor(cea[:, :, 0:n], ea[:, :, cols], post[:, 1:2, cols].to_broadcast([P, HG, n]),
                                           ALU.mult)
                    pool.drain().then_inc(pool_step, 1)
                    if k == NC:
                        weigh_x()
                        pool.tensor_tensor(bm, bc(bmask[:, :], P),
                                           btok[0:TS, :].unsqueeze(1).to_broadcast([TS, NB, P]), ALU.mult)
                        pool.drain().then_inc(bm_ready, 1)

                def group(g, s, u, rounds, late):
                    projects, scans = g is not None, s is not None
                    if scans:
                        side(s, 0)
                        side(s, 1)
                        if late:
                            hold(pool, st_st, 16 * s)
                            load_state(GROUPS - 1 if g is None else g - 1, s)
                        side(s, 2)
                        if projects:
                            hold(pool, cout_st, 16 * (L * GROUPS + g))
                    if projects:
                        pad_of(g, 0)
                        if scans:
                            low(L, u + AHEAD, rounds)
                    if scans:
                        side(s, 3)
                    if projects:
                        pad_of(g, 1)
                    if scans:
                        side(s, 4)
                        if projects:
                            low(L, u + 1 + AHEAD, rounds)
                        hold(pool, h_ready, 4 * s + 4)
                        pool.dma_start(row(A["hout"], s, "o p n -> (o p) n"), hst).then_inc(h_st, 16)
                        hold(pool, y_done, 5 * s + 5)
                        ends = ea[:, :, SEQ + NS - 1:T:NS].rearrange("p h b -> p b h")
                        for b in range(NB):
                            v = st[:, b, :].rearrange("p (h d) -> p h d", h=HG)
                            pool.tensor_tensor(v, v, bc(ends[:, b, :], HD), ALU.mult)
                        pool.drain().then_inc(st_dec, 1)
                    if projects:
                        pad_of(g, 2)
                        if scans:
                            low(L, u + 2 + AHEAD, rounds)
                        pad_of(g, 3)
                        load_decay(g, L * GROUPS + g)
                        if not scans:
                            load_state(g, L * GROUPS + g)
                        low(L, u + 3 + AHEAD, rounds)
                    if scans:
                        hold(pool, h_st, 16 * s + 16)
                        pool.sem_inc(h_free, 1)
                        hold(pool, ns_add, 4 * s + 4)
                        pool.dma_start(row(A["stout"], s, "o p b n -> (o p) b n"), st).then_inc(st_st, 16)
                    if projects:
                        low(L, u + 4 + AHEAD, rounds)
                        low(L, u + 5 + AHEAD, rounds)
                    else:
                        hold(pool, st_st, 16 * s + 16)
                        hold(pool, cout_st, 16 * s + 16)

                all_groups(pool, L, group)
                load_dt(L + 1)
                low(L, U_MRG + AHEAD)
                low(L, U_MRG + 1 + AHEAD)
                hold(pool, yssm_ready, 16 * L + 16)

                def load_wab(m):
                    hold(pool, mrg_done, 8 * L + m + 1)
                    pool.dma_start(wab, row(A["wab"], L * KT + m, "o p k n -> (o p) k n")).then_inc(wab_ld, 16)
                    for k in range(2, 4):
                        low(L, U_MRG + k + AHEAD, m)

                with pool.Fori(0, KT - 1) as m:
                    load_wab(m)
                    for k in range(4, 6):
                        low(L, U_MRG + k + AHEAD, m)
                load_wab(KT - 1)
                with pool.Fori(0, (UNITS - U_WO) // SLOTS - 1) as i:
                    for k in range(SLOTS):
                        low(L, U_WO + k + AHEAD, i)
                for u in range(UNITS - SLOTS + AHEAD, UNITS):
                    low(L, u)
                for u in range(AHEAD):
                    low(L + 1, u)
    return nc


def rotary_tables():
    half = ROPE // 2
    inv = np.power(np.float32(THETA), -np.arange(half, dtype=np.float32) / half).astype(np.float32)
    pos = np.concatenate([np.arange(SEQ), np.tile(PAST + np.arange(NS), NB)]).astype(np.float32)
    ang = (pos[:, None] * inv[None, :]).astype(np.float32)
    cos, sin = np.ones((P, T), np.float32), np.zeros((P, T), np.float32)
    swap = np.zeros((P, P), np.float32)
    for head in range(2):
        for d in range(half):
            a, b = 64 * head + d, 64 * head + half + d
            cos[a] = cos[b] = np.cos(ang[:, d])
            sin[a] = sin[b] = np.sin(ang[:, d])
            swap[b, a], swap[a, b] = -1.0, 1.0
    return cos, sin, swap


def attention_masks():
    m = np.full((P, RES, KEYS), NEG, np.float32)
    i = np.arange(P)[:, None]
    for r in range(RES):
        q, j = RES * i + r, np.arange(SEQ)[None, :]
        m[:, r, 0:SEQ][(q >= j) & (q - j <= 128)] = 0
        j = np.arange(P)[None, :]
        m[:, r, SEQ:SEQ + P][i >= j] = 0
        m[:, r, SEQ + P:KEYS][(i >= j) & ((i - j) % 4 == 0)] = 0
    s = np.full((NB, HG, NS, SKEYS), NEG, np.float32)
    for b in range(NB):
        for t in range(NS):
            s[b, :, t, 0:SEQ][:, np.arange(SEQ) % 4 == t] = 0
            s[b, :, t, SEQ:SEQ + P][:, np.arange(P) >= t] = 0
            s[b, :, t, SEQ + P:KEYS][:, np.arange(P) % 4 == t] = 0
            s[b, :, t, KEYS + NS * b:KEYS + NS * b + t + 1] = 0
            for g in (1, 2):
                s[b, :, t, KEYS + TS * g + NS * b + t] = 0
    return tuple((a.view(np.uint32) >> 16).astype(np.uint16) for a in (m, s.reshape(P, SKEYS)))


def kernel(**inputs):
    import concourse.bacc as bacc
    from concourse.bass_utils import run_bass_kernel_spmd

    i = {k: np.asarray(v) for k, v in inputs.items()}
    f32 = np.float32

    def tiles(w):
        k, n = w.shape
        return w.reshape(k // D, KT, P, n // P, P).transpose(3, 0, 2, 1, 4).reshape(n // P, k // D, P, KT * P)

    units = np.empty((DEPTH, UNITS, P, KT * P), f32)
    for l in range(DEPTH):
        w = i["w_in"][l]
        q, k, v = (tiles(w[:, o:o + AW])[:, 0] for o in (OFF_Q, OFF_K, OFF_V))
        z, xs = tiles(w[:, 0:D_IN])[:, 0], tiles(w[:, OFF_XBC:OFF_XBC + D_IN])[:, 0]
        bb = tiles(w[:, OFF_XBC + D_IN:OFF_XBC + D_IN + D])[:, 0]
        cc = tiles(w[:, OFF_XBC + D_IN + D:OFF_DT])[:, 0]
        gs, ga = tiles(w[:, OFF_G:OFF_G + D])[:, 0], tiles(w[:, OFF_G + D:])[:, 0]
        br = tiles(i["w_ssm_br"][l])
        u = [x for j in range(6) for x in (q[j], k[j], v[j])]
        u += [x for g in range(GROUPS) for x in (bb[g], cc[g], xs[2 * g], xs[2 * g + 1], z[2 * g], z[2 * g + 1])]
        u += [x for m in range(KT) for x in (gs[m], ga[m], br[m, 0], br[m, 1])]
        u += list(tiles(i["w_o"][l])[:, 0])
        up, down = tiles(i["w_up"][l])[:, 0], tiles(i["w_down"][l])
        for f in range(2):
            u += list(up[FT * f:FT * (f + 1)])
            u += [x for m in range(KT) for x in (down[m, 2 * f], down[m, 2 * f + 1])]
        for n, x in enumerate(u):
            units[l, n] = x

    def cols(v):
        return v.reshape(DEPTH, -1, P).transpose(0, 2, 1)

    conv_cols = np.concatenate([i["conv_w"], i["conv_b"][:, None]], 1)
    conv_cols = conv_cols.reshape(DEPTH, CW + 1, CONV // P, P).transpose(0, 3, 2, 1)
    skip = cols(np.repeat(i["d_skip"], HD, axis=1))
    gain = cols(i["ssm_norm_g"])
    order = [(16 + g, 24 + g, 2 * g, 2 * g + 1) for g in range(GROUPS)]
    par = np.empty((DEPTH, P, GROUPS, NGP), f32)
    for g, t in enumerate(order):
        par[:, :, g, 0:16] = conv_cols[:, :, list(t), 0:CW].reshape(DEPTH, P, 16)
        par[:, :, g, 16:20] = conv_cols[:, :, list(t), CW]
        par[:, :, g, 20:22] = skip[:, :, 2 * g:2 * g + 2]
        par[:, :, g, 22:24] = gain[:, :, 2 * g:2 * g + 2]
    flat = [t for ts in order for t in ts]
    cst = i["state_conv"].reshape(DEPTH, NB, CW - 1, CONV // P, P).transpose(0, 4, 3, 1, 2)[:, :, flat]
    kv128, kv512, kv2048 = (i[n] for n in ("cache_kv_w128", "cache_kv_w512", "cache_kv_w2048"))
    kv2048 = kv2048.reshape(DEPTH, NB, PAST // 16, 16, 2, HG, HD)[:, :, :, 0:4].reshape(DEPTH, NB, P, 2, HG, HD)
    cache = np.concatenate([kv512, kv128, kv2048], axis=2)
    kc = cache[:, :, :, 0].reshape(DEPTH, NB, KEYS, 2, P).transpose(0, 1, 4, 3, 2).reshape(DEPTH * NB, P, 2 * KEYS)
    vc = cache[:, :, :, 1].reshape(DEPTH, NB, 6, P, 256).transpose(0, 1, 3, 2, 4).reshape(DEPTH * NB, P, 6 * 256)
    st = i["state_ssm"].reshape(DEPTH, NB, GROUPS, 256, NST).transpose(0, 2, 4, 1, 3).reshape(DEPTH * GROUPS, P, NB, 256)
    x0 = np.concatenate([i["x_prompt"].reshape(SEQ, D), i["x_sample"].reshape(TS, D)])
    x0 = x0.reshape(T, KT, P).transpose(2, 1, 0)
    wdt = i["w_in"][:, :, OFF_DT:OFF_Q].reshape(DEPTH, KT, P, HEADS).transpose(0, 2, 1, 3)
    wab = i["w_attn_br"].reshape(DEPTH, 2, P, KT, P).transpose(0, 3, 2, 1, 4).reshape(DEPTH * KT, P, 2, P)
    lnp = np.concatenate([cols(i[n]) for n in ("ln1_g", "ln1_b", "ln2_g", "ln2_b")], axis=2)
    hpar = np.stack([i["dt_bias"], i["a_log"]], axis=2)
    wdt, hpar = (np.concatenate([a, a[:1]]) for a in (wdt, hpar))
    cos, sin, swap = rotary_tables()
    mask, mask_s = attention_masks()
    tok = np.arange(TS)
    restart = np.ones((HEADS, T), f32)
    restart[:, 0:SEQ:CHUNK] = 0
    restart[:, SEQ:T:NS] = 0
    arrays = {
        "x0": x0, "wst": units.reshape(DEPTH * UNITS, P, KT * P), "wdt": wdt, "wab": wab, "par": par, "lnp": lnp,
        "hpar": hpar, "cst": cst.reshape(DEPTH, P, 4 * GROUPS, NB * (CW - 1)), "kc": kc, "vc": vc, "st": st,
        "ident": np.eye(P, dtype=f32), "swap": swap, "cos": cos, "sin": sin,
        "tri": np.triu(np.ones((P, P), f32)),
        "tri_s": ((tok[:, None] // NS == tok[None, :] // NS) & (tok[:, None] <= tok[None, :])).astype(f32),
        "bmask": (tok[:, None] // NS == np.arange(NB)[None, :]).astype(f32), "restart": restart,
        "mask": mask.reshape(P, RES, KEYS), "mask_s": mask_s,
    }
    outs = {"y": (P, KT, T), "kv": (DEPTH, P, 12, T), "cout": (DEPTH * GROUPS, P, 4, 35),
            "hout": (DEPTH * GROUPS, P, 256), "stout": (DEPTH * GROUPS, P, NB, 256)}
    nc = bacc.Bacc("TRN2", target_bir_lowering=False, num_devices=1)
    feed, A = {}, {}
    for name, a in arrays.items():
        feed[f"in_{name}"] = np.ascontiguousarray(a)
        A[name] = nc.dram_tensor(f"in_{name}", a.shape, mybir.dt.from_np(a.dtype), kind="ExternalInput").ap()
    for name, shape in outs.items():
        A[name] = nc.dram_tensor(f"out_{name}", shape, F32, kind="ExternalOutput").ap()
    A["ac"] = nc.dram_tensor("scratch_ac", (HEADS, T), F32, kind="Internal").ap()
    build(nc, A)
    r = run_bass_kernel_spmd(nc, [feed], core_ids=[0]).results[0]
    y, kv, cout, hout, stout = (np.asarray(r[f"out_{n}"]) for n in outs)

    y = y.transpose(2, 1, 0).reshape(T, D)
    kv = kv.reshape(DEPTH, P, 2, 3, 2, T).transpose(3, 0, 5, 2, 4, 1)
    kv = kv.reshape(3, DEPTH, T, 2, HG, HD)
    kv_p = [kv[j, :, SEQ - min(w, SEQ):SEQ].reshape(DEPTH, 1, min(w, SEQ), 2, HG, HD) for j, (w, _) in enumerate(WINDOWS)]
    kv_s = [kv[j, :, SEQ:T].reshape(DEPTH, NB, NS, 2, HG, HD) for j in range(3)]
    cout = cout.reshape(DEPTH, GROUPS, P, 4, 35).transpose(0, 4, 1, 3, 2).reshape(DEPTH, 35, 4 * GROUPS, P)
    conv = np.empty((DEPTH, 35, CONV // P, P), f32)
    conv[:, :, flat] = cout
    conv = conv.reshape(DEPTH, 35, CONV)
    conv_s = conv[:, 3:].reshape(DEPTH, NB, NS, CONV)[:, :, 1:]
    ssm_p = hout.reshape(DEPTH, 1, GROUPS, P, HG, HD).transpose(0, 1, 2, 4, 5, 3).reshape(DEPTH, 1, HEADS, HD, NST)
    ssm_s = stout.reshape(DEPTH, GROUPS, P, NB, HG, HD).transpose(0, 3, 1, 4, 5, 2).reshape(DEPTH, NB, HEADS, HD, NST)
    return (y[0:SEQ].reshape(1, SEQ, D), y[SEQ:T].reshape(NB, NS, D), *kv_p, conv[:, 0:3].reshape(DEPTH, 1, 3, CONV),
            np.ascontiguousarray(ssm_p), *kv_s, np.ascontiguousarray(conv_s), np.ascontiguousarray(ssm_s))
```
